# Optimizing a Trainium2 kernel written in Bass

```python
import jax, jax.numpy as jnp
from jax import lax
import numpy as np

D_MODEL = 2048
BATCH = 1
SEQ = 256
DEPTH = 1

CHUNK = 64

D_MIX = D_MODEL
D_LRU = D_MIX // 2
D_POOL = D_MIX - D_LRU
LRU_HEADS = 16
LRU_HEAD_DIM = D_LRU // LRU_HEADS
CONV_WIDTH = 4
LRU_C = 8.0
POOL_WINDOWS = (2, 4, 8, 16)
POOL_GROUPS = len(POOL_WINDOWS)
POOL_GROUP_DIM = D_POOL // POOL_GROUPS
D_FF = ((8 * D_MODEL + 3 * 256 - 1) // (3 * 256)) * 256
N_MOD = 6
EPS = 1e-6


def rmsnorm(x, g):
    xf = x.astype(jnp.float32)
    y = xf * lax.rsqrt(jnp.mean(xf * xf, axis=-1, keepdims=True) + EPS)
    return (y * g.astype(jnp.float32)).astype(x.dtype)

def modulate(h, shift, scale):
    return h * (1 + scale[:, None, :]) + shift[:, None, :]

def causal_dwconv(x, w, b):
    y = lax.conv_general_dilated(
        x, w[:, None, :].astype(x.dtype), window_strides=(1,),
        padding=[(CONV_WIDTH - 1, 0)],
        dimension_numbers=("NWC", "WIO", "NWC"),
        feature_group_count=x.shape[-1])
    return y + b.astype(x.dtype)

def rg_lru(x, w_a, b_a, w_i, b_i, lam):
    bsz, seq, _ = x.shape
    xf = x.astype(jnp.float32)
    xh = xf.reshape(bsz, seq, LRU_HEADS, LRU_HEAD_DIM)
    r = jax.nn.sigmoid(jnp.einsum("bshi,hij->bshj", xh, w_a.astype(jnp.float32)).reshape(bsz, seq, D_LRU)
                       + b_a.astype(jnp.float32))
    i = jax.nn.sigmoid(jnp.einsum("bshi,hij->bshj", xh, w_i.astype(jnp.float32)).reshape(bsz, seq, D_LRU)
                       + b_i.astype(jnp.float32))
    log_a = LRU_C * r * jax.nn.log_sigmoid(lam.astype(jnp.float32))
    a = jnp.exp(log_a)
    mult = jnp.sqrt(-jnp.expm1(2.0 * log_a))
    u = mult * (i * xf)

    def combine(left, right):
        a1, b1 = left
        a2, b2 = right
        return a1 * a2, a2 * b1 + b2

    _, h = lax.associative_scan(combine, (a, u), axis=1)
    return h

def pool_mixer(x, w_pool, ls_pool):
    bsz, seq, _ = x.shape
    xf = x.astype(jnp.float32)
    cs0 = jnp.concatenate([jnp.zeros((bsz, 1, D_POOL), jnp.float32), jnp.cumsum(xf, axis=1)], axis=1)
    pos1 = jnp.arange(1, seq + 1, dtype=jnp.float32)
    outs = []
    for g, w in enumerate(POOL_WINDOWS):
        sl = slice(g * POOL_GROUP_DIM, (g + 1) * POOL_GROUP_DIM)
        c0 = cs0[..., sl]
        upper = c0[:, 1:]
        lower = jnp.concatenate([jnp.zeros((bsz, w - 1, POOL_GROUP_DIM), jnp.float32),
                                 c0[:, :seq - w + 1]], axis=1)
        count = jnp.minimum(pos1, float(w))[None, :, None]
        outs.append((upper - lower) / count - xf[..., sl])
    pooled = jnp.stack(outs, axis=2)
    y = jnp.einsum("bsgc,gcd->bsgd", pooled, w_pool.astype(jnp.float32)) * ls_pool.astype(jnp.float32)
    return y.reshape(bsz, seq, D_POOL)

def first_inputs(seed: int = 0) -> dict:
    key = jax.random.key(seed)
    ks = jax.random.split(key, 24)
    f32 = jnp.float32
    nrm = lambda k, shape, s: jax.random.normal(k, shape, f32) * s
    a0 = jax.random.uniform(ks[12], (DEPTH, D_LRU), f32, 0.9, 0.999)
    s0 = a0 ** (1.0 / LRU_C)
    lam = jnp.log(s0) - jnp.log1p(-s0)
    return {
        "x": nrm(ks[0], (BATCH, SEQ, D_MODEL), 1.0),
        "c": nrm(ks[1], (BATCH, D_MODEL), 1.0),
        "w_ada": nrm(ks[2], (DEPTH, D_MODEL, N_MOD * D_MODEL), 0.5 * D_MODEL ** -0.5),
        "b_ada": nrm(ks[3], (DEPTH, N_MOD * D_MODEL), 0.02),
        "g_norm_mix": 1.0 + nrm(ks[4], (DEPTH, D_MODEL), 0.05),
        "w_in": nrm(ks[5], (DEPTH, D_MODEL, 2 * D_LRU + D_POOL), D_MODEL ** -0.5),
        "w_conv": nrm(ks[6], (DEPTH, CONV_WIDTH, D_LRU), CONV_WIDTH ** -0.5),
        "b_conv": nrm(ks[7], (DEPTH, D_LRU), 0.02),
        "w_rg_a": nrm(ks[8], (DEPTH, LRU_HEADS, LRU_HEAD_DIM, LRU_HEAD_DIM), LRU_HEAD_DIM ** -0.5),
        "b_rg_a": nrm(ks[9], (DEPTH, D_LRU), 0.02),
        "w_rg_i": nrm(ks[10], (DEPTH, LRU_HEADS, LRU_HEAD_DIM, LRU_HEAD_DIM), LRU_HEAD_DIM ** -0.5),
        "b_rg_i": nrm(ks[11], (DEPTH, D_LRU), 0.02),
        "lru_lambda": lam,
        "w_pool": nrm(ks[13], (DEPTH, POOL_GROUPS, POOL_GROUP_DIM, POOL_GROUP_DIM), POOL_GROUP_DIM ** -0.5),
        "ls_pool": 1.0 + nrm(ks[14], (DEPTH, POOL_GROUPS, POOL_GROUP_DIM), 0.1),
        "w_out": nrm(ks[15], (DEPTH, D_MIX, D_MODEL), D_MIX ** -0.5),
        "g_norm_ffn": 1.0 + nrm(ks[16], (DEPTH, D_MODEL), 0.05),
        "w_ffn_gate": nrm(ks[17], (DEPTH, D_MODEL, D_FF), D_MODEL ** -0.5),
        "w_ffn_up": nrm(ks[18], (DEPTH, D_MODEL, D_FF), D_MODEL ** -0.5),
        "w_ffn_down": nrm(ks[19], (DEPTH, D_FF, D_MODEL), D_FF ** -0.5),
        "g_norm_final": 1.0 + nrm(ks[20], (D_MODEL,), 0.05),
    }

def first_block(x, c, w_ada, b_ada, g_norm_mix, w_in, w_conv, b_conv, w_rg_a, b_rg_a,
              w_rg_i, b_rg_i, lru_lambda, w_pool, ls_pool, w_out, g_norm_ffn,
              w_ffn_gate, w_ffn_up, w_ffn_down, g_norm_final):
    dt = x.dtype
    c_act = jax.nn.silu(c)
    for l in range(DEPTH):
        mod = c_act @ w_ada[l] + b_ada[l]
        sh1, sc1, gt1, sh2, sc2, gt2 = jnp.split(mod, N_MOD, axis=-1)

        h = modulate(rmsnorm(x, g_norm_mix[l]), sh1, sc1)
        proj = h @ w_in[l]
        xr = proj[..., :D_LRU]
        gr = proj[..., D_LRU:2 * D_LRU]
        xp = proj[..., 2 * D_LRU:]
        xr = causal_dwconv(xr, w_conv[l], b_conv[l])
        hr = rg_lru(xr, w_rg_a[l], b_rg_a[l], w_rg_i[l], b_rg_i[l], lru_lambda[l])
        y_lru = (hr * jax.nn.gelu(gr.astype(jnp.float32))).astype(dt)
        y_pool = pool_mixer(xp, w_pool[l], ls_pool[l]).astype(dt)
        y = jnp.concatenate([y_lru, y_pool], axis=-1) @ w_out[l]
        x = x + gt1[:, None, :] * y

        h = modulate(rmsnorm(x, g_norm_ffn[l]), sh2, sc2)
        f = (jax.nn.silu(h @ w_ffn_gate[l]) * (h @ w_ffn_up[l])) @ w_ffn_down[l]
        x = x + gt2[:, None, :] * f
    return rmsnorm(x, g_norm_final)


RET_HEADS = 4
RET_HEAD_DIM = 256
RET_WIDTH = RET_HEADS * RET_HEAD_DIM
RET_CHUNK = 128
RET_ROPE_THETA = 10000.0
MOBA_HEADS = 8
MOBA_HEAD_DIM = 128
MOBA_WIDTH = MOBA_HEADS * MOBA_HEAD_DIM
MOBA_BLOCK = 256
MOBA_TOPK = 3
MOBA_Q_CHUNK = 64
ROPE_THETA = 500000.0
ROT_DIM = MOBA_HEAD_DIM // 4
D_FF_2 = 5632
CONV_WIDTH_2 = 3
IN_SIZES = (RET_WIDTH, RET_WIDTH, RET_WIDTH, RET_WIDTH,
            MOBA_WIDTH, MOBA_WIDTH, MOBA_WIDTH,
            D_MODEL, D_MODEL)
IN_TOTAL = sum(IN_SIZES)


def rmsnorm_2(x, w):
    xf = x.astype(jnp.float32)
    y = xf * lax.rsqrt(jnp.mean(xf * xf, axis=-1, keepdims=True) + EPS)
    return (y * w.astype(jnp.float32)).astype(x.dtype)

def rotary(x, rot_dim, theta):
    S = x.shape[1]
    pos = jnp.arange(S, dtype=jnp.float32)
    inv_freq = jnp.asarray(theta, jnp.float32) ** (-jnp.arange(0, rot_dim, 2, dtype=jnp.float32) / rot_dim)
    ang = pos[:, None] * inv_freq[None, :]
    cos = jnp.cos(ang)[None, :, None, :]
    sin = jnp.sin(ang)[None, :, None, :]
    xr = x[..., :rot_dim].astype(jnp.float32)
    x1, x2 = jnp.split(xr, 2, axis=-1)
    rot = jnp.concatenate([x1 * cos - x2 * sin, x2 * cos + x1 * sin], axis=-1).astype(x.dtype)
    return jnp.concatenate([rot, x[..., rot_dim:]], axis=-1)

def retention(q, k, v):
    B, S, H, dk = q.shape
    dv = v.shape[-1]
    C = RET_CHUNK
    N = S // C
    q = q.astype(jnp.float32)
    k = k.astype(jnp.float32) * (dk ** -0.5)
    v = v.astype(jnp.float32)
    log_g = jnp.log1p(-jnp.exp2(-5.0 - jnp.arange(H, dtype=jnp.float32)))
    i = jnp.arange(C, dtype=jnp.float32)
    diff = i[:, None] - i[None, :]
    causal = diff >= 0
    decay = jnp.where(causal[None], jnp.exp(log_g[:, None, None] * jnp.where(causal, diff, 0.0)[None]), 0.0)
    xi = jnp.exp(log_g[:, None] * (i[None, :] + 1.0))
    zeta = jnp.exp(log_g[:, None] * (C - 1.0 - i[None, :]))
    g_chunk = jnp.exp(log_g * C)

    def to_chunks(t):
        return t.reshape(B, N, C, H, t.shape[-1]).transpose(1, 0, 3, 2, 4)

    def step(state, xs):
        qc, kc, vc = xs
        scores = jnp.einsum('bhqd,bhkd->bhqk', qc, kc) * decay[None]
        inner = jnp.einsum('bhqk,bhkd->bhqd', scores, vc)
        cross = jnp.einsum('bhqd,bhde->bhqe', qc, state) * xi[None, :, :, None]
        new_state = state * g_chunk[None, :, None, None] + jnp.einsum(
            'bhkd,bhke->bhde', kc * zeta[None, :, :, None], vc)
        return new_state, inner + cross

    init = jnp.zeros((B, H, dk, dv), jnp.float32)
    _, out = lax.scan(step, init, (to_chunks(q), to_chunks(k), to_chunks(v)))
    return out.transpose(1, 0, 3, 2, 4).reshape(B, S, H, dv)

def moba_attention(q, k, v):
    B, S, H, d = q.shape
    dtype = q.dtype
    BS = MOBA_BLOCK
    Cq = MOBA_Q_CHUNK
    NB = -(-S // BS)
    S_pad = NB * BS
    NQ = S // Cq
    topk = min(MOBA_TOPK, NB)
    scale = d ** -0.5
    qh = q.transpose(0, 2, 1, 3)
    pad = ((0, 0), (0, 0), (0, S_pad - S), (0, 0))
    kb = jnp.pad(k.transpose(0, 2, 1, 3), pad).reshape(B, H, NB, BS, d)
    vb = jnp.pad(v.transpose(0, 2, 1, 3), pad).reshape(B, H, NB, BS, d)
    kmean = jnp.mean(kb.astype(jnp.float32), axis=3)
    q_all = qh.reshape(B, H, NQ, Cq, d).transpose(0, 2, 1, 3, 4).reshape(B * NQ, H, Cq, d)
    b_idx = jnp.repeat(jnp.arange(B, dtype=jnp.int32), NQ)
    n_idx = jnp.tile(jnp.arange(NQ, dtype=jnp.int32), B)
    hh = jnp.arange(H)[:, None, None]

    def step(args):
        qc, b, n = args
        kb_b, vb_b, km_b = kb[b], vb[b], kmean[b]
        q0 = n * Cq
        cb = q0 // BS
        qpos = q0 + jnp.arange(Cq)
        bscore = jnp.einsum('hqd,hnd->hqn', qc.astype(jnp.float32), km_b)
        past = jnp.arange(NB) < cb
        bscore = jnp.where(past[None, None, :], bscore, -jnp.inf)
        _, idx = lax.top_k(bscore, topk)
        valid = idx < cb
        k_sel = kb_b[hh, idx]
        v_sel = vb_b[hh, idx]
        s_sel = jnp.einsum('hqd,hqnkd->hqnk', qc, k_sel, preferred_element_type=jnp.float32) * scale
        s_sel = jnp.where(valid[..., None], s_sel, -jnp.inf).reshape(H, Cq, topk * BS)
        k_own = lax.dynamic_index_in_dim(kb_b, cb, axis=1, keepdims=False)
        v_own = lax.dynamic_index_in_dim(vb_b, cb, axis=1, keepdims=False)
        s_own = jnp.einsum('hqd,hkd->hqk', qc, k_own, preferred_element_type=jnp.float32) * scale
        kpos = cb * BS + jnp.arange(BS)
        s_own = jnp.where((kpos[None, :] <= qpos[:, None])[None], s_own, -jnp.inf)
        p = jax.nn.softmax(jnp.concatenate([s_sel, s_own], axis=-1), axis=-1).astype(dtype)
        p_sel = p[..., :topk * BS].reshape(H, Cq, topk, BS)
        p_own = p[..., topk * BS:]
        o = jnp.einsum('hqnk,hqnkd->hqd', p_sel, v_sel) + jnp.einsum('hqk,hkd->hqd', p_own, v_own)
        return o.astype(dtype)

    out = lax.map(step, (q_all, b_idx, n_idx))
    return out.reshape(B, NQ, H, Cq, d).transpose(0, 1, 3, 2, 4).reshape(B, S, H * d)

def causal_dwconv_2(u, w, b):
    S = u.shape[1]
    up = jnp.pad(u, ((0, 0), (CONV_WIDTH_2 - 1, 0), (0, 0)))
    y = b
    for j in range(CONV_WIDTH_2):
        y = y + w[j] * up[:, j:j + S]
    return y

def second_inputs(seed: int = 0) -> dict:
    key = jax.random.key(seed)
    ks = jax.random.split(key, 14)
    f32 = jnp.float32

    def normal(k, shape, scale):
        return jax.random.normal(k, shape, f32) * scale

    def gain(k, shape):
        return 1.0 + 0.05 * jax.random.normal(k, shape, f32)

    return {
        "x": jax.random.normal(ks[0], (BATCH, SEQ, D_MODEL), f32),
        "attn_norm_w": gain(ks[1], (DEPTH, D_MODEL)),
        "w_in": normal(ks[2], (DEPTH, D_MODEL, IN_TOTAL), D_MODEL ** -0.5),
        "ret_norm_w": gain(ks[3], (DEPTH, RET_WIDTH)),
        "w_ret_up": normal(ks[4], (DEPTH, RET_WIDTH, D_MODEL), RET_WIDTH ** -0.5),
        "w_moba_up": normal(ks[5], (DEPTH, MOBA_WIDTH, D_MODEL), MOBA_WIDTH ** -0.5),
        "w_out": normal(ks[6], (DEPTH, D_MODEL, D_MODEL), D_MODEL ** -0.5),
        "ffn_norm_w": gain(ks[7], (DEPTH, D_MODEL)),
        "w_ffn_up": normal(ks[8], (DEPTH, D_MODEL, 2 * D_FF_2), D_MODEL ** -0.5),
        "conv_w": normal(ks[9], (DEPTH, CONV_WIDTH_2, 2 * D_FF_2), CONV_WIDTH_2 ** -0.5),
        "conv_b": normal(ks[10], (DEPTH, 2 * D_FF_2), 0.01),
        "w_ffn_down": normal(ks[11], (DEPTH, D_FF_2, D_MODEL), D_FF_2 ** -0.5),
        "final_norm_w": gain(ks[12], (D_MODEL,)),
    }

def second_block(x, attn_norm_w, w_in, ret_norm_w, w_ret_up, w_moba_up, w_out,
              ffn_norm_w, w_ffn_up, conv_w, conv_b, w_ffn_down, final_norm_w):
    B, S, _ = x.shape
    split_at = [int(s) for s in np.cumsum(IN_SIZES)[:-1]]
    for l in range(DEPTH):
        h = rmsnorm_2(x, attn_norm_w[l])
        proj = h @ w_in[l]
        rq, rk, rv, rg, mq, mk, mv, g_ret, g_moba = jnp.split(proj, split_at, axis=-1)
        rq = rotary(rq.reshape(B, S, RET_HEADS, RET_HEAD_DIM), RET_HEAD_DIM, RET_ROPE_THETA)
        rk = rotary(rk.reshape(B, S, RET_HEADS, RET_HEAD_DIM), RET_HEAD_DIM, RET_ROPE_THETA)
        rv = rv.reshape(B, S, RET_HEADS, RET_HEAD_DIM)
        o_ret = retention(rq, rk, rv)
        o_ret = o_ret * lax.rsqrt(jnp.mean(o_ret * o_ret, axis=-1, keepdims=True) + EPS)
        o_ret = o_ret.reshape(B, S, RET_WIDTH).astype(x.dtype) * ret_norm_w[l]
        o_ret = jax.nn.silu(rg) * o_ret
        mq = rotary(mq.reshape(B, S, MOBA_HEADS, MOBA_HEAD_DIM), ROT_DIM, ROPE_THETA)
        mk = rotary(mk.reshape(B, S, MOBA_HEADS, MOBA_HEAD_DIM), ROT_DIM, ROPE_THETA)
        mv = mv.reshape(B, S, MOBA_HEADS, MOBA_HEAD_DIM)
        o_moba = moba_attention(mq, mk, mv)
        merged = jax.nn.sigmoid(g_ret) * (o_ret @ w_ret_up[l]) + jax.nn.sigmoid(g_moba) * (o_moba @ w_moba_up[l])
        x = x + merged @ w_out[l]
        h2 = rmsnorm_2(x, ffn_norm_w[l])
        up = causal_dwconv_2(h2 @ w_ffn_up[l], conv_w[l], conv_b[l])
        a, b = jnp.split(up, 2, axis=-1)
        x = x + (jax.nn.silu(a) * b) @ w_ffn_down[l]
    return rmsnorm_2(x, final_norm_w)


def setup_inputs(seed=0):
    out = dict(first_inputs(seed))
    for name, value in second_inputs(seed + 1).items():
        if name != "x":
            out[name + "_2"] = value
    return out


def reference(
    x, c, w_ada, b_ada, g_norm_mix, w_in, w_conv, b_conv, w_rg_a, b_rg_a, w_rg_i, b_rg_i,
    lru_lambda, w_pool, ls_pool, w_out, g_norm_ffn, w_ffn_gate, w_ffn_up, w_ffn_down,
    g_norm_final, attn_norm_w_2, w_in_2, ret_norm_w_2, w_ret_up_2, w_moba_up_2, w_out_2,
    ffn_norm_w_2, w_ffn_up_2, conv_w_2, conv_b_2, w_ffn_down_2, final_norm_w_2,
):
    x = first_block(
        x, c, w_ada, b_ada, g_norm_mix, w_in, w_conv, b_conv, w_rg_a, b_rg_a, w_rg_i, b_rg_i,
        lru_lambda, w_pool, ls_pool, w_out, g_norm_ffn, w_ffn_gate, w_ffn_up, w_ffn_down,
        g_norm_final,
    )
    return second_block(
        x, attn_norm_w_2, w_in_2, ret_norm_w_2, w_ret_up_2, w_moba_up_2, w_out_2, ffn_norm_w_2,
        w_ffn_up_2, conv_w_2, conv_b_2, w_ffn_down_2, final_norm_w_2,
    )


_drawn_inputs = setup_inputs


def setup_inputs(seed=0):
    import zlib

    import numpy as np

    out = dict(_drawn_inputs(seed))
    spreads = {}
    factors = {'g_norm_mix': 3.073,
     'b_conv': 3.804,
     'b_rg_a': 8.0,
     'b_rg_i': 8.0,
     'g_norm_ffn': 3.075,
     'ret_norm_w_2': 3.356,
     'conv_b_2': 8.0}
    for name, (base, spread) in spreads.items():
        noise = np.random.default_rng([zlib.crc32(name.encode()), seed]).standard_normal(out[name].shape)
        drawn = base * np.exp(spread * noise) if base else spread * noise
        out[name] = __import__('jax').numpy.asarray(drawn.astype(out[name].dtype))
    for name, factor in factors.items():
        out[name] = (out[name] * factor).astype(out[name].dtype)
    return out
```

```python
from contextlib import ExitStack

import concourse.bass as bass
import concourse.mybir as mybir
import numpy as np

F32 = mybir.dt.float32
F32R = mybir.dt.float32r
ACT = mybir.ActivationFunctionType
ALU = mybir.AluOpType
AX = mybir.AxisListType

P = 128
T = 256
D = 2048
DB = D // P
SLAB = 256
CHUNKS = 4
KT = DB // CHUNKS
RAW = 8
RING = 4
EPS = 1e-6

D_LRU = D // 2
LRU_HEAD = 64
LB = D_LRU // P
CONV = 4
LRU_C = 8.0
WINDOWS = (2, 4, 8, 16)
D_FF = 5632
FB = D_FF // P
N_MOD = 6
FFN_GROUPS = (8, 8, 6)

RET_HEADS, RET_DIM, RET_THETA = 4, 256, 10000.0
MOBA_HEADS, MOBA_DIM, MOBA_THETA = 8, 128, 500000.0
ROT = MOBA_DIM // 4
CONV_2 = 3
BIG = 3.0e38

IN_SLABS = (2 * D_LRU + D_LRU) // SLAB
OUT_SLABS = D // SLAB
IN2_SLABS = (4 * 1024 + 3 * 1024 + 2 * D) // SLAB

ADA_COLS = 1024
ADA_PARTS = N_MOD * D // ADA_COLS
ADA_FIRST = 6
ADA_RING = 8
RIDE_RING = 3
RIDES = [3] * IN_SLABS + [CHUNKS] * 15
RIDE_AT = [(S, c) for S, n in enumerate(RIDES) for c in range(n)]
assert len(RIDE_AT) == (ADA_PARTS - ADA_FIRST) * DB

IN2_ORDER = [*range(16, 28), *range(0, 16), *range(28, 44)]
V_SLABS = [*range(8, 12), *range(20, 24)]

PARAMS = {}
_at = 0
for _name, _rows in (
    ("c", DB), ("b_ada", N_MOD * DB), ("g_norm_mix", DB), ("w_conv", CONV * LB), ("b_conv", LB), ("b_rg_a", LB),
    ("b_rg_i", LB), ("lru_lambda", LB), ("ls_pool", LB), ("g_norm_ffn", DB), ("g_norm_final", DB),
    ("attn_norm_w_2", DB), ("ret_norm_w_2", LB), ("ffn_norm_w_2", DB), ("conv_w_2", CONV_2 * 2 * FB),
    ("conv_b_2", 2 * FB), ("final_norm_w_2", DB),
):
    PARAMS[_name] = (_at, _rows)
    _at += _rows
N_PARAMS = _at


class Steps:

    def __init__(self):
        self.base, self.done = 0, 0

    def next(self):
        self.done += 1
        return self.base + self.done

    def enter(self, i, per):
        self.outer, self.per = self.base + self.done, per
        self.base, self.done = self.outer + i * per, 0

    def leave(self, turns):
        assert self.done == self.per, (self.done, self.per)
        self.base, self.done = self.outer + turns * self.per, 0


def build(nc, dram, out):
    ctx = ExitStack()

    def at(name, shape, offset, dt=F32):
        return nc.alloc_sbuf_tensor_at(name, shape, dt, offset=offset)

    top = 16512
    def place(size):
        nonlocal top
        where, top = top, top + size
        return where

    raw = at("raw", [P, RAW, KT, SLAB], place(RAW * KT * SLAB * 4))
    split = at("split", [P, RING, KT, 2, SLAB], place(RING * KT * 2 * SLAB * 4), F32R)
    H_AT = place(DB * 2 * T * 4)
    h_s = at("h_s", [P, DB, 2, T], H_AT, F32R)
    MID = place(DB * 2 * T * 4)
    x_t = at("x_t", [P, DB, T], place(DB * T * 4))
    low = at("low", [P, 2, 2, T], place(2 * 2 * T * 4))
    val_at = place(2 * 2 * T * 4)
    val = at("val", [P, 2, 2, T], val_at)
    val4 = at("val4", [P, 4, T], val_at)
    par = at("par", [P, N_PARAMS], place(N_PARAMS * 4))
    mod = at("mod", [P, N_MOD * DB], place(N_MOD * DB * 4))
    ident = at("ident", [P, P], place(P * 4))
    ones = at("ones", [P, P], place(P * 4))
    gain = at("gain", [P, DB], place(DB * 4))
    c_act = at("c_act", [P, DB], place(DB * 4))
    lam_e = at("lam_e", [P, LB], place(32))
    lam_z = at("lam_z", [P, LB], place(32))
    lam_q = at("lam_q", [P, LB], place(32))
    lam_p = at("lam_p", [P, LB], place(32))
    lam_8 = at("lam_8", [P, LB], place(32))
    lam_n8 = at("lam_n8", [P, LB], place(32))
    inv_n = at("inv_n", [P, 16], place(64))
    s_max = at("s_max", [P, 2], place(32))
    s_neg = at("s_neg", [P, 2], place(32))
    s_sum = at("s_sum", [P, 2], place(32))
    s_inv = at("s_inv", [P, 2], place(32))
    SSQ = place(2048)
    ssq = at("ssq", [P, 2, T], SSQ)
    RSTD = place(1024)
    rstd = at("rstd", [P, T], RSTD)
    F = place(0)

    mid_s = at("mid_s", [P, DB, 2, T], MID, F32R)
    rg_a = at("rg_a", [P, LB, P], MID)
    rg_i = at("rg_i", [P, LB, P], MID + 4096)
    gelu = at("gelu", [P, LB, T], MID + 8192)
    gate_r = at("gate_r", [P, LB, T], MID + 16384)
    gate_i = at("gate_i", [P, LB, T], MID + 24576)
    qk_r = at("qk_r", [P, RET_HEADS, 2, 2, T], MID)
    o_r = at("o_r", [P, LB, 2, T], MID, F32R)
    v_r = at("v_r", [P, 2, 1024], MID + 16384)
    g_r = at("g_r", [P, LB, T], MID + 24576)
    sig_m = at("sig_m", [P, DB, T], MID + 16384)

    acc = at("acc", [P, 2, ADA_COLS], F)
    ride = at("ride", [P, RIDE_RING, ADA_COLS], F + 8192)
    ada = at("ada", [P, ADA_RING, ADA_COLS], H_AT)
    w_pool = at("w_pool_sb", [P, 4, 2, 256], F + 20480)
    PAD = CONV - 1
    xr_pad = at("xr_pad", [P, LB, PAD + T], F + 28672)
    lru_t = at("lru_t", [P, LB, T], F + 28672)
    xc = at("xc", [P, LB, T], F + 36960)
    WPAD = 16
    pool_x = at("pool_x", [P, 2, WPAD + T], F + 45152)
    pool_a = at("pool_a", [P, 2, WPAD + T], F + 45152 + 2176)
    pool_b = at("pool_b", [P, 2, WPAD + T], SSQ)

    qk_m = at("qk_m", [P, MOBA_HEADS, 2, T], F)
    o_m = at("o_m", [P, MOBA_HEADS, 2, T], F, F32R)
    v_m = at("v_m", [P, 2, 1024], F + 16384)
    sig_r = at("sig_r", [P, DB, T], F + 16384)
    rope_r = at("rope_r", [P, 2, T], F + 32768)
    rope_m = at("rope_m", [ROT, 2, T], F + 34816)
    decay = at("decay", [P, RET_HEADS, T], F + 36864)
    cmask = at("cmask", [P, 3 * P], F + 40960)
    prob = at("prob", [P, 2, 3 * P], F + 42496)
    prob_t = at("prob_t", [P, 3 * P], F + 45568)
    perm = at("perm", [ROT, ROT], F + 47104)
    PAD_2 = CONV_2 - 1
    up_pad = at("up_pad", [P, 2, 2, PAD_2 + T], F)
    conv_o = at("conv_o", [P, 2, 2, T], F + 4352)
    out_t = at("out_t", [P, DB, T], MID)
    assert F + 49504 <= nc.sbuf_usable_end, (F + 49504, nc.sbuf_usable_end)

    def col(name, k=0, n=1):
        a = PARAMS[name][0] + k
        return par[:, a:a + n]

    ps = ctx.enter_context(nc.psum_tensor("ps", [P, 2, 2, 512], F32))
    pm = [ctx.enter_context(nc.psum_tensor(f"pm{k}", [P, 512], F32)) for k in range(4)]

    def sem(name):
        return ctx.enter_context(nc.semaphore(name))

    raw_loaded = [sem(f"raw_loaded{k}") for k in range(RAW)]
    hi_ready = sem("hi_ready")
    lo_ready = sem("lo_ready")
    chunk_used = sem("chunk_used")
    low_copied = sem("low_copied")
    evacuated = sem("evacuated")
    params_loaded = sem("params_loaded")
    x_loaded = sem("x_loaded")
    side_loaded = sem("side_loaded")
    tables_loaded = sem("tables_loaded")
    ident_loaded = sem("ident_loaded")
    constants = sem("constants")
    ada_loaded = [sem(f"ada_loaded{k}") for k in range(ADA_RING)]
    ride_loaded = [sem(f"ride_loaded{k}") for k in range(RIDE_RING)]
    c_ready = sem("c_ready")
    ada_added = sem("ada_added")
    ada_turned = sem("ada_turned")
    mod_ready = sem("mod_ready")
    squared = sem("squared")
    x_updated = sem("x_updated")
    ssq_added = sem("ssq_added")
    ssq_summed = sem("ssq_summed")
    var_ready = sem("var_ready")
    std_ready = sem("std_ready")
    norm_t = sem("norm_t")
    norm_hi = sem("norm_hi")
    h_ready = sem("h_ready")
    lam_exp = sem("lam_exp")
    lam_abs = sem("lam_abs")
    lam_ready = sem("lam_ready")
    conv_ready = sem("conv_ready")
    gates_mm = sem("gates_mm")
    gates_read = sem("gates_read")
    decays = sem("decays")
    mult_sq = sem("mult_sq")
    mult_ready = sem("mult_ready")
    gelu_ready = sem("gelu_ready")
    y_full = sem("y_full")
    y_hi = sem("y_hi")
    y_ready = sem("y_ready")
    pooled = sem("pooled")
    pool_mm = sem("pool_mm")
    pool_full = sem("pool_full")
    pool_hi = sem("pool_hi")
    pool_ready = sem("pool_ready")
    val_ready = sem("val_ready")
    act_done = sem("act_done")
    mid_ready = sem("mid_ready")
    qkv_stored = sem("qkv_stored")
    swapped = sem("swapped")
    rotated = sem("rotated")
    scores_mm = sem("scores_mm")
    maxed = sem("maxed")
    exped = sem("exped")
    prob_ready = sem("prob_ready")
    turned = sem("turned")
    prob_copied = sem("prob_copied")
    moba_mm = sem("moba_mm")
    moba_hi = sem("moba_hi")
    moba_ready = sem("moba_ready")
    ret_scores = sem("ret_scores")
    ret_decayed = sem("ret_decayed")
    ret_mm = sem("ret_mm")
    ret_squared = sem("ret_squared")
    ret_summed = sem("ret_summed")
    ret_var = sem("ret_var")
    ret_std = sem("ret_std")
    ret_full = sem("ret_full")
    ret_hi = sem("ret_hi")
    ret_ready = sem("ret_ready")
    merged_t = sem("merged_t")
    merged_hi = sem("merged_hi")
    merged_ready = sem("merged_ready")
    out_ready = sem("out_ready")
    stored = sem("stored")
    dve_step = sem("dve_step")

    S_IN = 0
    S_OUT = S_IN + IN_SLABS
    S_FFN = S_OUT + OUT_SLABS
    FFN_SPAN = sum(2 * n + OUT_SLABS for n in FFN_GROUPS)
    S_IN2 = S_FFN + FFN_SPAN
    S_MERGE = S_IN2 + IN2_SLABS
    S_OUT2 = S_MERGE + OUT_SLABS
    S_FFN2 = S_OUT2 + OUT_SLABS
    S_END = S_FFN2 + FFN_SPAN

    def evac_count(S):
        return S + (OUT_SLABS if S >= S_OUT2 else 0)

    def groups(first):
        S, pairs = first, 0
        for g, n in enumerate(FFN_GROUPS):
            yield g, S, n, S + 2 * n, 2 * n // CHUNKS, pairs
            S += 2 * n + OUT_SLABS
            pairs += n

    def tiles_of(S):
        for first in (S_FFN, S_FFN2):
            for _, _, _, down, kt, _ in groups(first):
                if down <= S < down + OUT_SLABS:
                    return kt
        return KT

    block = ctx.enter_context(nc.Block())

    @block.sync
    def _(sp):
        sp.dma_start(par[:, :], dram["params"]).then_inc(params_loaded, 16)

        def load(pair, c, src, kt=KT):
            if not (isinstance(pair, int) and pair == 0):
                sp.wait_ge(lo_ready, 2 * CHUNKS * pair + c - RAW + 1)
            sp.dma_start(raw[:, c, 0:kt, :].rearrange("p k n -> p (k n)"), src).then_inc(raw_loaded[c], 16)

        def chunk(w, slab, c):
            return w[bass.ds(slab, 1), c].rearrange("a p n -> p (a n)")

        for part in range(2):
            for k in range(DB):
                if part * DB + k >= ADA_RING:
                    sp.wait_ge(ada_added, part * DB + k - ADA_RING + 1)
                sp.dma_start(ada[:, k % ADA_RING, :], dram["w_ada"][k * P:(k + 1) * P, part * ADA_COLS:(part + 1) * ADA_COLS])\
                  .then_inc(ada_loaded[k % ADA_RING], 16)
            if part == 0:
                sp.dma_start(x_t[:, :, :], dram["x_fm"].rearrange("(b p) t -> p b t", p=P)).then_inc(x_loaded, 16)
        with sp.Fori(2, ADA_FIRST) as part:
            for k in range(DB):
                sp.wait_ge(ada_added, part * DB + k - ADA_RING + 1)
                sp.dma_start(ada[:, k % ADA_RING, :], dram["w_ada"][k * P:(k + 1) * P, bass.ds(part * ADA_COLS, ADA_COLS)])\
                  .then_inc(ada_loaded[k % ADA_RING], 16)
        for c in range(2 * CHUNKS):
            load(0, c, dram["w_in"][c // CHUNKS, c % CHUNKS])

        done_pairs = -(-(len(RIDES) * CHUNKS + RAW) // (2 * CHUNKS))
        for G in range(RAW, done_pairs * 2 * CHUNKS):
            at_slab = ((G - RAW) // CHUNKS, (G - RAW) % CHUNKS)
            if at_slab in RIDE_AT:
                piece = RIDE_AT.index(at_slab)
                part, k = ADA_FIRST + piece // DB, piece % DB
                if piece >= RIDE_RING:
                    sp.wait_ge(ada_added, ADA_FIRST * DB + piece - RIDE_RING + 1)
                sp.dma_start(ride[:, piece % RIDE_RING, :],
                             dram["w_ada"][k * P:(k + 1) * P, part * ADA_COLS:(part + 1) * ADA_COLS])\
                  .then_inc(ride_loaded[piece % RIDE_RING], 16)
            S, c = G // CHUNKS, G % CHUNKS
            if S < S_OUT:
                src = dram["w_in"][S, c]
            elif S < S_FFN:
                src = dram["w_out"][S - S_OUT, c]
            else:
                src = (dram["w_ffn_gate"], dram["w_ffn_up"])[S % 2][(S - S_FFN) // 2, c]
            load(S // 2, CHUNKS * (S % 2) + c, src)

        def stream_ffn(wa, wb, wd, first, done):
            for g, gu, n, down, kt, pairs in groups(first):
                if g == 0 and done == n:
                    pass
                else:
                  with sp.Fori(done if g == 0 else 0, n) as i:
                    for c in range(2 * CHUNKS):
                        load(i + gu // 2, c, chunk((wa, wb)[c // CHUNKS], i + pairs, c % CHUNKS))
                with sp.Fori(0, OUT_SLABS // 2) as i:
                    for c in range(2 * CHUNKS):
                        load(i + down // 2, c, chunk(wd[g], i * 2 + c // CHUNKS, c % CHUNKS), kt)

        stream_ffn(dram["w_ffn_gate"], dram["w_ffn_up"], [dram[f"w_ffn_down{g}"] for g in range(3)], S_FFN,
                   done_pairs - S_FFN // 2)
        with sp.Fori(0, IN2_SLABS // 2) as i:
            for c in range(2 * CHUNKS):
                load(i + S_IN2 // 2, c, chunk(dram["w_in_2"], i * 2 + c // CHUNKS, c % CHUNKS))
        with sp.Fori(0, OUT_SLABS // 2) as i:
            for c in range(2 * CHUNKS):
                w = (dram["w_ret_up_2"], dram["w_moba_up_2"])[c // 2 % 2]
                load(i + S_MERGE // 2, c, chunk(w, i * 2 + c // CHUNKS, c % 2))
        with sp.Fori(0, OUT_SLABS // 2) as i:
            for c in range(2 * CHUNKS):
                load(i + S_OUT2 // 2, c, chunk(dram["w_out_2"], i * 2 + c // CHUNKS, c % CHUNKS))
        stream_ffn(dram["w_ffn_a_2"], dram["w_ffn_b_2"], [dram[f"w_ffn_down_2{g}"] for g in range(3)], S_FFN2, 0)

        for j in range(4):
            sp.wait_ge(out_ready, 4 * (j + 1))
            sp.dma_start(out.rearrange("(b p) t -> p b t", p=P)[:, 4 * j:4 * j + 4, :], out_t[:, 4 * j:4 * j + 4, :])\
              .then_inc(stored, 16)
        sp.wait_ge(stored, 64)

    @block.gpsimd
    def _(pool):
        pool.memset(ones[:, :], 1.0).then_inc(constants, 1)
        pool.memset(rg_a[:, :, :], 0.0).then_inc(constants, 1)
        pool.memset(rg_i[:, :, :], 0.0).then_inc(constants, 1)
        pool.memset(xr_pad[:, :, 0:PAD], 0.0).then_inc(constants, 1)
        pool.memset(pool_x[:, :, 0:WPAD], 0.0).then_inc(constants, 1)
        pool.memset(pool_a[:, :, 0:WPAD], 0.0).then_inc(constants, 1)
        for n in range(16):
            pool.memset(inv_n[:, n:n + 1], 1.0 / (n + 1)).then_inc(constants, 1)
        pool.dma_start(ident[:, :], dram["ident"]).then_inc(ident_loaded, 16)
        pool.dma_start(w_pool[:, :, :, :], dram["w_pool"].rearrange("g (k p) n -> p g k n", p=P)).then_inc(side_loaded, 16)
        pool.wait_ge(constants, 3)
        for w, sb in ((dram["w_rg_a"], rg_a), (dram["w_rg_i"], rg_i)):
            for k in range(2):
                pool.dma_start(sb[64 * k:64 * k + 64, :, 64 * k:64 * k + 64], w[k].rearrange("h i j -> i h j"))\
                    .then_inc(side_loaded, 16)
        pool.wait_ge(chunk_used, CHUNKS * S_FFN)
        pool.dma_start(rope_r[:, :, :], dram["rope_r"]).then_inc(tables_loaded, 16)
        pool.dma_start(rope_m[:, :, :], dram["rope_m"]).then_inc(tables_loaded, 16)
        pool.dma_start(decay[:, :, :], dram["decay"]).then_inc(tables_loaded, 16)
        pool.dma_start(cmask[:, :], dram["cmask"]).then_inc(tables_loaded, 16)
        pool.dma_start(perm[:, :], dram["perm"]).then_inc(tables_loaded, 16)

    @block.tensor
    def _(pe):
        def slab(S, s, acts, kt=KT, guard=None, tok=False):
            if not (isinstance(S, int) and S < 2):
                pe.wait_ge(evacuated, evac_count_of(S) - 1)
            for c in range(CHUNKS):
                if guard is not None:
                    guard(c)
                multiply(CHUNKS * S + c, c, s, acts, c * kt, kt, c == 0, c == CHUNKS - 1, tok)

        def multiply(G, slot, s, acts, k0, kt, first, last, tok=False):
            pe.wait_ge(lo_ready, G + 1)
            for k in range(kt):
                start, stop = first and k == 0, last and k == kt - 1
                for b in range(2):
                    if tok:
                        pe.matmul(ps[:, s, b, :], acts[:, k0 + k, 0, b * P:(b + 1) * P],
                                  split[:, slot, k, :, :].rearrange("p h n -> p (h n)"), start=start, stop=False)
                        mm = pe.matmul(ps[:, s, b, 0:SLAB], acts[:, k0 + k, 1, b * P:(b + 1) * P],
                                       split[:, slot, k, 0, :], start=False, stop=stop)
                    else:
                        pe.matmul(ps[:, s, b, :], split[:, slot, k, 0, b * P:(b + 1) * P],
                                  acts[:, k0 + k, :, :].rearrange("p h t -> p (h t)"), start=start, stop=False)
                        mm = pe.matmul(ps[:, s, b, 0:T], split[:, slot, k, 1, b * P:(b + 1) * P],
                                       acts[:, k0 + k, 0, :], start=False, stop=stop)
            mm.then_inc(chunk_used, 1)

        offset = [0]

        def evac_count_of(S):
            return S + offset[0]

        def turn_ada(part, parity):
            pe.wait_ge(ada_added, (part + 1) * DB)
            for j in range(8):
                mm = pe.matmul(pm[3][:, 8 * parity + j:8 * parity + j + 1], acc[:, parity, j * P:(j + 1) * P],
                               ones[:, 0:1], start=True, stop=True)
            mm.then_inc(ada_turned, 1)

        def turn_rides(S):
            for part in range(ADA_FIRST, ADA_PARTS):
                if RIDE_AT[(part - ADA_FIRST + 1) * DB - 1][0] + 1 == S:
                    turn_ada(part, part % 2)

        def sum_squares(n):
            pe.wait_ge(ssq_added, OUT_SLABS * (n + 1))
            pe.matmul(pm[2][:, 0:T], ones[:, :], ssq[:, 0, :], start=True, stop=False)
            pe.matmul(pm[2][:, 0:T], ones[:, :], ssq[:, 1, :], start=False, stop=True).then_inc(ssq_summed, 1)

        def normed(k):
            def guard(c):
                pe.wait_ge(h_ready, DB * k + KT * (c + 1))
            return guard

        pe.wait_ge(constants, 1)
        turn_ada(0, 0)
        turn_ada(1, 1)
        sum_squares(0)
        with pe.Fori(1, ADA_FIRST // 2) as i:
            for parity in range(2):
                pe.wait_ge(mod_ready, i * 2 + (parity - 1))
                turn_ada(i * 2 + parity, parity)

        def gates(q):
            pe.wait_ge(conv_ready, q + 1)
            if q == 0:
                pe.wait_ge(side_loaded, 16 * 5)
            if q >= 1:
                pe.wait_ge(gates_read, q)
            for b in range(2):
                blk = 2 * q + b
                pe.matmul(pm[b][:, 0:T], rg_a[:, blk, :], xc[:, blk, :], start=True, stop=True)
                mm = pe.matmul(pm[b][:, T:2 * T], rg_i[:, blk, :], xc[:, blk, :], start=True, stop=True)
            mm.then_inc(gates_mm, 1)

        def pool_product(g):
            pe.wait_ge(pooled, g + 1)
            if g >= 1:
                pe.wait_ge(pool_full, g)
            for b in range(2):
                for k in range(2):
                    mm = pe.matmul(pm[2][:, b * T:(b + 1) * T], w_pool[:, g, k, b * P:(b + 1) * P],
                                   val[:, g % 2, k, :], start=(k == 0), stop=(k == 1))
            mm.then_inc(pool_mm, 1)

        for q in range(IN_SLABS):
            slab(S_IN + q, q % 2, h_s, guard=normed(0) if q == 0 else None)
            if 1 <= q <= 4:
                gates(q - 1)
            if q >= 9:
                pool_product(q - 9)
            turn_rides(S_IN + q)
        pool_product(3)

        def mixed(c):
            if c < 2:
                pe.wait_ge(y_ready, c + 1)
            else:
                pe.wait_ge(pool_ready, 2 * (c - 1))
        for q in range(OUT_SLABS):
            slab(S_OUT + q, q % 2, mid_s, guard=mixed if q == 0 else None)
            turn_rides(S_OUT + q)
        sum_squares(1)

        def ffn(first, k_h, n_sq):
            for g, gu, n, down, kt, pairs in groups(first):
                done = 0
                if g == 0:
                    done = (len(RIDES) + 2 - S_FFN) // 2 if first == S_FFN else 1
                    for i in range(done):
                        for s in range(2):
                            slab(gu + 2 * i + s, s, h_s, guard=normed(k_h) if i + s == 0 else None)
                            turn_rides(gu + 2 * i + s)
                with pe.Fori(done, n) as i:
                    slab(i * 2 + gu, 0, h_s)
                    slab(i * 2 + gu + 1, 1, h_s)

                def hidden(c):
                    pe.wait_ge(mid_ready, (first == S_FFN2) * (FB // 2) + pairs + -(-kt * (c + 1) // 2))
                slab(down, 0, mid_s, kt, guard=hidden)
                slab(down + 1, 1, mid_s, kt)
                with pe.Fori(1, OUT_SLABS // 2) as i:
                    slab(i * 2 + down, 0, mid_s, kt)
                    slab(i * 2 + down + 1, 1, mid_s, kt)
            sum_squares(n_sq)

        ffn(S_FFN, 1, 2)
        sum_squares(3)

        def swap(j):
            pe.wait_ge(qkv_stored, j + 1)
            if j == 0:
                pe.wait_ge(tables_loaded, 16 * 5)
            if j >= 1:
                pe.wait_ge(rotated, j)
            pe.matmul(pm[0][0:ROT, :], perm[:, :], qk_m[0:ROT, 2 * (j % 4):2 * (j % 4) + 2, j // 4, :],
                      start=True, stop=True).then_inc(swapped, 1)

        def moba_scores(h):
            pe.wait_ge(rotated, 8)
            if h >= 1:
                pe.wait_ge(maxed, h)
            pe.matmul(pm[1][:, 0:P], qk_m[:, h, 0, 0:P], qk_m[:, h, 1, 0:P], start=True, stop=True)
            pe.matmul(pm[1][:, P:3 * P], qk_m[:, h, 0, P:T], qk_m[:, h, 1, :], start=True, stop=True)\
              .then_inc(scores_mm, 1)

        def moba_turn(h):
            pe.wait_ge(prob_ready, h + 1)
            if h >= 1:
                pe.wait_ge(prob_copied, h)
            pe.wait_ge(ident_loaded, 16)
            for j in range(3):
                mm = pe.transpose(pm[2][:, j * P:(j + 1) * P], prob[:, h % 2, j * P:(j + 1) * P], ident[:, :])
            mm.then_inc(turned, 1)

        def moba_out(h):
            pe.wait_ge(prob_copied, h + 1)
            pe.wait_ge(qkv_stored, 12)
            if h >= 1:
                pe.wait_ge(moba_ready, h)
            pe.matmul(pm[3][:, 0:T], v_m[:, 0, h * P:(h + 1) * P], prob_t[:, 0:T], start=True, stop=False)
            pe.matmul(pm[3][:, P:T], v_m[:, 1, h * P:(h + 1) * P], prob_t[:, T:3 * P], start=False, stop=True)\
              .then_inc(moba_mm, 1)

        def ret_score(h):
            pe.wait_ge(qkv_stored, 12 + 8)
            if h >= 1:
                pe.wait_ge(ret_decayed, h)
            for k in range(2):
                pe.matmul(pm[0][:, 0:T], qk_r[:, h, 1, k, 0:P], qk_r[:, h, 0, k, :], start=(k == 0), stop=(k == 1))
            for k in range(2):
                mm = pe.matmul(pm[0][:, T:3 * P], qk_r[:, h, 1, k, P:T], qk_r[:, h, 0, k, P:T],
                               start=(k == 0), stop=(k == 1))
            mm.then_inc(ret_scores, 1)

        def ret_out(h):
            pe.wait_ge(ret_decayed, h + 1)
            pe.wait_ge(qkv_stored, 12 + 8 + h + 1)
            if h >= 1:
                pe.wait_ge(ret_full, h)
            for e in range(2):
                c0 = h * RET_DIM + e * P
                pe.matmul(pm[1][:, e * T:(e + 1) * T], v_r[:, 0, c0:c0 + P], prob[:, h % 2, 0:T], start=True, stop=False)
                mm = pe.matmul(pm[1][:, e * T + P:(e + 1) * T], v_r[:, 1, c0:c0 + P], prob[:, h % 2, T:3 * P],
                               start=False, stop=True)
            mm.then_inc(ret_mm, 1)

        def ret_sum(h):
            pe.wait_ge(ret_squared, h + 1)
            if h >= 1:
                pe.wait_ge(ret_var, h)
            pe.matmul(pm[2][:, 0:T], ones[:, :], val[:, 0, 0, :], start=True, stop=False)
            pe.matmul(pm[2][:, 0:T], ones[:, :], val[:, 0, 1, :], start=False, stop=True).then_inc(ret_summed, 1)

        for q in range(IN2_SLABS):
            slab(S_IN2 + q, q % 2, h_s, guard=normed(2) if q == 0 else None, tok=q in V_SLABS)
            if 1 <= q <= 8:
                swap(q - 1)
            if 0 <= q - 15 < 8:
                moba_out(q - 15)
            if 0 <= q - 14 < 8:
                moba_turn(q - 14)
            if 0 <= q - 12 < 8:
                moba_scores(q - 12)
            if 23 <= q <= 29 and q % 2 == 1:
                ret_score((q - 23) // 2)
            if 24 <= q <= 30 and q % 2 == 0:
                ret_out((q - 24) // 2)
            if 25 <= q <= 31 and q % 2 == 1:
                ret_sum((q - 25) // 2)

        pe.wait_ge(ret_ready, RET_HEADS)
        pe.wait_ge(moba_ready, MOBA_HEADS)
        with pe.Fori(0, OUT_SLABS) as m:
            for s, acts in ((0, o_r), (1, o_m)):
                pe.wait_ge(evacuated, m * 2 + S_MERGE + s - 1)
                for c in range(2):
                    multiply(m * CHUNKS + CHUNKS * S_MERGE + 2 * s + c, 2 * s + c, s, acts, c * KT, KT, c == 0, c == 1)
        offset[0] = OUT_SLABS

        def merged(c):
            pe.wait_ge(merged_ready, 2 * (c + 1))
        for q in range(2):
            slab(S_OUT2 + q, q, h_s, guard=merged if q == 0 else None)
        with pe.Fori(1, OUT_SLABS // 2) as i:
            slab(i * 2 + S_OUT2, 0, h_s)
            slab(i * 2 + S_OUT2 + 1, 1, h_s)
        sum_squares(4)
        ffn(S_FFN2, 3, 5)

    @block.scalar
    def _(act):
        def convert(pair, s, c, kt=KT):
            G = 2 * CHUNKS * pair + CHUNKS * s + c
            act.wait_ge(raw_loaded[CHUNKS * s + c], 16 * (pair + 1))
            if not (isinstance(pair, int) and G < RING):
                act.wait_ge(chunk_used, G - RING + 1)
            act.activation(split[:, c, 0:kt, 0, :], raw[:, CHUNKS * s + c, 0:kt, :], ACT.Copy).then_inc(hi_ready, 1)

        def copy_low(E, s, used):
            act.wait_ge(chunk_used, used)
            if not (isinstance(E, int) and E < 2):
                act.wait_ge(evacuated, E - 1)
            act.activation(low[:, s, :, :], ps[:, s, :, T:2 * T], ACT.Copy).then_inc(low_copied, 1)

        offset = [0]

        def turn(pair, s, mid=None, kt_next=KT):
            for c in range(CHUNKS):
                if s == 0:
                    convert(pair, 1, c, kt_next)
                else:
                    convert(pair + 1, 0, c, kt_next)
                if mid is not None:
                    mid(c)
            S = 2 * pair + s
            copy_low(S + offset[0], s, CHUNKS * S + CHUNKS)

        def last_turn(pair, s):
            S = 2 * pair + s
            copy_low(S + offset[0], s, CHUNKS * S + CHUNKS)

        def square(n, j):
            act.wait_ge(x_updated, OUT_SLABS * (n - 1) + j + 1)
            act.activation(val[:, j % 2, :, :], x_t[:, 2 * j:2 * j + 2, :], ACT.Square).then_inc(squared, 1)

        def root(n):
            act.wait_ge(var_ready, n + 1)
            act.activation(rstd[:, :], rstd[:, :], ACT.Sqrt).then_inc(std_ready, 1)

        def norm(n, k, shift):
            root(n)
            for b in range(DB):
                act.wait_ge(norm_t, DB * k + b + 1)
                if shift is None:
                    act.activation(h_s[:, b, 0, :], val4[:, b % 4, :], ACT.Copy).then_inc(norm_hi, 1)
                else:
                    act.activation(h_s[:, b, 0, :], val4[:, b % 4, :], ACT.Identity,
                                   bias=mod[:, shift * DB + b:shift * DB + b + 1]).then_inc(norm_hi, 1)

        act.wait_ge(params_loaded, 16)
        act.activation(c_act[:, :], col("c", 0, DB), ACT.Silu).then_inc(c_ready, 1)
        act.wait_ge(x_loaded, 16)
        for j in range(OUT_SLABS):
            if j >= 2:
                act.wait_ge(ssq_added, j - 1)
            act.activation(val[:, j % 2, :, :], x_t[:, 2 * j:2 * j + 2, :], ACT.Square).then_inc(squared, 1)
        act.wait_ge(lam_abs, 1)
        act.activation(lam_e[:, :], lam_p[:, :], ACT.Exp, scale=-1.0).then_inc(lam_exp, 1)
        for c in range(CHUNKS):
            convert(0, 0, c)
        norm(0, 0, 0)

        def sigmoids(q):
            act.wait_ge(gates_mm, q + 1)
            for b in range(2):
                blk = 2 * q + b
                act.activation(gate_r[:, blk, :], pm[b][:, 0:T], ACT.Sigmoid, bias=col("b_rg_a", blk))
                last = act.activation(gate_i[:, blk, :], pm[b][:, T:2 * T], ACT.Sigmoid, bias=col("b_rg_i", blk))
            last.then_inc(gates_read, 1)

        def lru_decay(half):
            if half == 0:
                act.wait_ge(lam_ready, 1)
                act.wait_ge(gates_read, 4)
                act.wait_ge(conv_ready, 4)
            for blk in range(4 * half, 4 * half + 4):
                act.activation(lru_t[:, blk, :], gate_r[:, blk, :], ACT.Tanh, scale=lam_n8[:, blk:blk + 1])
            for blk in range(4 * half, 4 * half + 4):
                last = act.activation(gate_r[:, blk, :], gate_r[:, blk, :], ACT.Exp, scale=lam_8[:, blk:blk + 1])
            last.then_inc(decays, 1)

        def first_mid(q):
            def mid(c):
                if c == 0 and 2 <= q <= 5:
                    sigmoids(q - 2)
                if c == 0 and q in (6, 7):
                    lru_decay(q - 6)
                if c == 0 and q == 8:
                    act.wait_ge(evacuated, 8)
                    act.activation(gelu[:, :, :], gelu[:, :, :], ACT.Gelu_apprx_tanh).then_inc(gelu_ready, 1)
                if c == 0 and q in (9, 10):
                    half = q - 9
                    act.wait_ge(mult_sq, half + 1)
                    act.activation(lru_t[:, 4 * half:4 * half + 4, :], lru_t[:, 4 * half:4 * half + 4, :], ACT.Sqrt)\
                       .then_inc(mult_ready, 1)
                if c == 0 and q == 11:
                    y_high(0)
                if c == 3 and q >= 10:
                    pool_high(q - 10)
            return mid

        def y_high(half):
            act.wait_ge(y_full, half + 1)
            act.activation(mid_s[:, 4 * half:4 * half + 4, 0, :], xc[:, 4 * half:4 * half + 4, :], ACT.Copy)\
               .then_inc(y_hi, 1)

        def pool_high(g):
            act.wait_ge(pool_full, g + 1)
            act.wait_ge(y_full, min(g + 1, 2))
            act.activation(mid_s[:, LB + 2 * g:LB + 2 * g + 2, 0, :], val[:, g % 2, :, :], ACT.Copy).then_inc(pool_hi, 1)

        for q in range(IN_SLABS):
            turn(q // 2, q % 2, mid=first_mid(q))
        y_high(1)
        pool_high(2)
        pool_high(3)
        for q in range(OUT_SLABS):
            turn((S_OUT + q) // 2, q % 2)
            square(1, q)
        norm(1, 1, 3)

        def ffn(first, n_sq):
            for g, gu, n, down, kt, pairs in groups(first):
                def hidden_pair(i, kt_next=KT):
                    pair = i + gu // 2
                    turn(pair, 0)
                    if first == S_FFN:
                        act.wait_ge(evacuated, pair * 2 + 1)
                        act.activation(val[:, 0, :, :], val[:, 0, :, :], ACT.Silu).then_inc(act_done, 1)
                    else:
                        act.wait_ge(val_ready, i + (pairs + 1))
                        act.activation(conv_o[:, 0, :, :], conv_o[:, 0, :, :], ACT.Silu).then_inc(act_done, 1)
                    turn(pair, 1, kt_next=kt_next)
                with act.Fori(0, n - 1) as i:
                    hidden_pair(i)
                hidden_pair(n - 1, kt)
                last_group = g == len(FFN_GROUPS) - 1
                if not last_group:
                    with act.Fori(0, OUT_SLABS // 2) as i:
                        turn(i + down // 2, 0)
                        turn(i + down // 2, 1)
                else:
                    for q in range(OUT_SLABS):
                        if q < OUT_SLABS - 1:
                            turn((down + q) // 2, q % 2, kt_next=kt)
                        elif down + q + 1 < S_END:
                            turn((down + q) // 2, q % 2)
                        else:
                            last_turn((down + q) // 2, q % 2)
                        square(n_sq, q)

        ffn(S_FFN, 2)
        root(2)
        for q in range(OUT_SLABS):
            square(3, q)
        norm(3, 2, None)

        def moba_exp(h):
            act.wait_ge(maxed, h + 1)
            act.activation(prob[:, h % 2, 0:P], prob[:, h % 2, 0:P], ACT.Exp, bias=s_neg[:, 0:1], scale=MOBA_DIM ** -0.5,
                           accum_out=s_sum[:, 0:1])
            act.activation(prob[:, h % 2, P:3 * P], prob[:, h % 2, P:3 * P], ACT.Exp, bias=s_neg[:, 1:2], scale=MOBA_DIM ** -0.5,
                           accum_out=s_sum[:, 1:2]).then_inc(exped, 1)

        def moba_copy(h):
            act.wait_ge(turned, h + 1)
            if h >= 1:
                act.wait_ge(moba_mm, h)
            act.activation(prob_t[:, :], pm[2][:, 0:3 * P], ACT.Copy).then_inc(prob_copied, 1)

        def moba_high(h):
            act.wait_ge(moba_mm, h + 1)
            act.activation(o_m[:, h, 0, :], pm[3][:, 0:T], ACT.Copy).then_inc(moba_hi, 1)

        def ret_square(h):
            act.wait_ge(ret_mm, h + 1)
            act.wait_ge(act_done, FB // 2 + min(2 * h + 1, 4) + max(2 * h - 3, 0))
            act.activation(val[:, 0, :, :].rearrange("p b t -> p (b t)"), pm[1][:, :], ACT.Square).then_inc(ret_squared, 1)

        def ret_root(h):
            act.wait_ge(ret_var, h + 1)
            act.activation(rstd[:, :], rstd[:, :], ACT.Sqrt).then_inc(ret_std, 1)

        def ret_high(h):
            act.wait_ge(ret_full, h + 1)
            act.activation(o_r[:, 2 * h:2 * h + 2, 0, :], val[:, 0, :, :], ACT.Copy).then_inc(ret_hi, 1)

        def second_mid(q):
            def mid(c):
                if c == 1 and 0 <= q - 13 < 8:
                    moba_exp(q - 13)
                if c == 0 and 0 <= q - 15 < 8:
                    moba_copy(q - 15)
                if c == 0 and 0 <= q - 16 < 8:
                    moba_high(q - 16)
                if 25 <= q <= 31 and q % 2 == 1 and c == 0:
                    ret_square((q - 25) // 2)
                if 26 <= q <= 32 and q % 2 == 0 and c == 0:
                    ret_root((q - 26) // 2)
                if 26 <= q <= 32 and q % 2 == 0 and c == 3:
                    ret_high((q - 26) // 2)
            return mid

        for q in range(IN2_SLABS):
            turn((S_IN2 + q) // 2, q % 2, mid=second_mid(q))
            if 24 <= q < 28:
                act.wait_ge(qkv_stored, q + 1)
                act.activation(g_r[:, 2 * (q - 24):2 * (q - 24) + 2, :], g_r[:, 2 * (q - 24):2 * (q - 24) + 2, :],
                               ACT.Silu).then_inc(act_done, 1)
            if q >= 28:
                k = q - 28
                sg, j = (sig_r, k) if k < 8 else (sig_m, k - 8)
                act.wait_ge(evacuated, S_IN2 + q + 1)
                act.activation(sg[:, 2 * j:2 * j + 2, :], val[:, q % 2, :, :], ACT.Sigmoid).then_inc(act_done, 1)

        for m in range(OUT_SLABS):
            pair, s = (S_MERGE + m) // 2, m % 2
            for c in range(CHUNKS):
                if s == 0:
                    convert(pair, 1, c)
                else:
                    convert(pair + 1, 0, c)
                if c == 1:
                    copy_low(S_MERGE + 2 * m, 0, CHUNKS * (S_MERGE + m) + 2)
            copy_low(S_MERGE + 2 * m + 1, 1, CHUNKS * (S_MERGE + m) + 4)
            act.wait_ge(merged_t, m + 1)
            act.activation(h_s[:, 2 * m:2 * m + 2, 0, :], val[:, 0, :, :], ACT.Copy).then_inc(merged_hi, 1)
        offset[0] = OUT_SLABS
        for q in range(OUT_SLABS):
            turn((S_OUT2 + q) // 2, q % 2)
            square(4, q)
        norm(4, 3, None)
        ffn(S_FFN2, 5)
        root(5)

    @block.vector
    def _(dve):
        steps = Steps()

        def own(ins):
            ins.then_inc(dve_step, 1)
            dve.wait_ge(dve_step, steps.next())

        def convert(pair, s, c, kt=KT):
            G = 2 * CHUNKS * pair + CHUNKS * s + c
            dve.wait_ge(hi_ready, G + 1)
            dve.tensor_tensor(split[:, c, 0:kt, 1, :], raw[:, CHUNKS * s + c, 0:kt, :],
                              split[:, c, 0:kt, 0, :].bitcast(F32), ALU.subtract).then_inc(lo_ready, 1)

        def evacuate(E, s, dst):
            dve.wait_ge(low_copied, E + 1)
            dve.tensor_tensor(dst, ps[:, s, :, 0:T], low[:, s, :, :], ALU.add).then_inc(evacuated, 1)
            dve.wait_ge(evacuated, E + 1)

        offset = [0]

        def turn(pair, s, dst, mid=None, kt_next=KT):
            for c in range(CHUNKS):
                if s == 0:
                    convert(pair, 1, c, kt_next)
                else:
                    convert(pair + 1, 0, c, kt_next)
                if mid is not None:
                    mid(c)
            evacuate(2 * pair + s + offset[0], s, dst)

        def add_ada(part, k, parity, piece, loaded, count):
            dve.wait_ge(loaded, 16 * count)
            if k == 0:
                if not (isinstance(part, int) and part < 2):
                    dve.wait_ge(ada_turned, part - 1)
                dve.tensor_scalar(acc[:, parity, :], piece, c_act[:, k:k + 1], None, ALU.mult).then_inc(ada_added, 1)
            else:
                dve.wait_ge(ada_added, part * DB + k)
                dve.scalar_tensor_tensor(out=acc[:, parity, :], in0=piece, scalar=c_act[:, k:k + 1],
                                         in1=acc[:, parity, :], op0=ALU.mult, op1=ALU.add).then_inc(ada_added, 1)

        def add_first(part, k, parity):
            slot = k % ADA_RING
            add_ada(part, k, parity, ada[:, slot, :], ada_loaded[slot], part * (DB // ADA_RING) + (k // ADA_RING + 1))

        def add_rides(S, c):
            if (S, c) in RIDE_AT:
                piece = RIDE_AT.index((S, c))
                part, k, slot = ADA_FIRST + piece // DB, piece % DB, piece % RIDE_RING
                add_ada(part, k, part % 2, ride[:, slot, :], ride_loaded[slot], piece // RIDE_RING + 1)

        def finish_ada(part, parity):
            dve.wait_ge(ada_turned, part + 1)
            a = PARAMS["b_ada"][0]
            dve.tensor_tensor(mod[:, bass.ds(part * 8, 8)], pm[3][:, 8 * parity:8 * parity + 8],
                              par[:, bass.ds(part * 8 + a, 8)], ALU.add).then_inc(mod_ready, 1)

        def finish_rides(S):
            for part in range(ADA_FIRST, ADA_PARTS):
                if RIDE_AT[(part - ADA_FIRST + 1) * DB - 1][0] + 2 == S:
                    finish_ada(part, part % 2)

        def add_squares(n, j):
            dve.wait_ge(squared, OUT_SLABS * n + j + 1)
            if j == 0:
                dve.tensor_copy(ssq[:, :, :], val[:, 0, :, :]).then_inc(ssq_added, 1)
            else:
                dve.wait_ge(ssq_added, OUT_SLABS * n + j)
                dve.tensor_tensor(ssq[:, :, :], ssq[:, :, :], val[:, j % 2, :, :], ALU.add).then_inc(ssq_added, 1)

        def inv_rms(n):
            dve.wait_ge(ssq_summed, n + 1)
            dve.tensor_scalar(rstd[:, :], pm[2][:, 0:T], 1.0 / D, EPS, ALU.mult, ALU.add).then_inc(var_ready, 1)
            dve.wait_ge(std_ready, n + 1)
            own(dve.reciprocal(rstd[:, :], rstd[:, :]))

        def norm(n, k, shift):
            inv_rms(n)

            def lo(b):
                dve.wait_ge(norm_hi, DB * k + b + 1)
                if shift is None:
                    dve.tensor_tensor(h_s[:, b, 1, :], val4[:, b % 4, :], h_s[:, b, 0, :].bitcast(F32), ALU.subtract)\
                       .then_inc(h_ready, 1)
                else:
                    dve.scalar_tensor_tensor(out=h_s[:, b, 1, :], in0=val4[:, b % 4, :],
                                             scalar=mod[:, shift * DB + b:shift * DB + b + 1],
                                             in1=h_s[:, b, 0, :].bitcast(F32), op0=ALU.add, op1=ALU.subtract)\
                       .then_inc(h_ready, 1)
            for b in range(DB):
                if b >= 4:
                    dve.wait_ge(h_ready, DB * k + b - 3)
                dve.scalar_tensor_tensor(out=val4[:, b % 4, :], in0=x_t[:, b, :], scalar=gain[:, b:b + 1],
                                         in1=rstd[:, :], op0=ALU.mult, op1=ALU.mult).then_inc(norm_t, 1)
                if b >= 1:
                    lo(b - 1)
            lo(DB - 1)
            dve.wait_ge(h_ready, DB * (k + 1))

        def residual(S, gate, k, dst_val):
            for b in range(2):
                xs = x_t[:, 2 * k + b, :]
                if gate is None:
                    ins = dve.tensor_tensor(xs, xs, dst_val[:, b, :], ALU.add)
                else:
                    ins = dve.scalar_tensor_tensor(out=xs, in0=dst_val[:, b, :],
                                                   scalar=mod[:, gate * DB + 2 * k + b:gate * DB + 2 * k + b + 1],
                                                   in1=xs, op0=ALU.mult, op1=ALU.add)
            return ins

        dve.wait_ge(params_loaded, 16)
        dve.wait_ge(c_ready, 1)
        for part in range(2):
            for k in range(DB):
                add_first(part, k, part)
                if part == 1 and k == 4:
                    finish_ada(0, 0)
        dve.wait_ge(x_loaded, 16)
        for j in range(OUT_SLABS):
            add_squares(0, j)
        lam = col("lru_lambda", 0, LB)
        dve.scalar_tensor_tensor(out=lam_p[:, :], in0=lam, scalar=-1.0, in1=lam, op0=ALU.mult, op1=ALU.max)\
           .then_inc(lam_abs, 1)
        dve.wait_ge(lam_exp, 1)
        own(dve.tensor_scalar(lam_z[:, :], lam_e[:, :], 2.0, None, ALU.add))
        own(dve.reciprocal(lam_z[:, :], lam_z[:, :]))
        own(dve.tensor_tensor(lam_z[:, :], lam_z[:, :], lam_e[:, :], ALU.mult))
        own(dve.tensor_tensor(lam_q[:, :], lam_z[:, :], lam_z[:, :], ALU.mult))
        own(dve.tensor_scalar(lam_p[:, :], lam_q[:, :], 1.0 / 17, None, ALU.mult))
        for n in (15, 13, 11, 9, 7, 5, 3):
            own(dve.scalar_tensor_tensor(out=lam_p[:, :], in0=lam_p[:, :], scalar=1.0 / n, in1=lam_q[:, :],
                                         op0=ALU.add, op1=ALU.mult))
        own(dve.scalar_tensor_tensor(out=lam_p[:, :], in0=lam_p[:, :], scalar=1.0, in1=lam_z[:, :],
                                     op0=ALU.add, op1=ALU.mult))
        own(dve.tensor_scalar(lam_e[:, :], lam, 0.0, None, ALU.min))
        own(dve.scalar_tensor_tensor(out=lam_z[:, :], in0=lam_p[:, :], scalar=-2.0, in1=lam_e[:, :],
                                     op0=ALU.mult, op1=ALU.add))
        own(dve.tensor_scalar(lam_8[:, :], lam_z[:, :], LRU_C, None, ALU.mult))
        dve.tensor_scalar(lam_n8[:, :], lam_z[:, :], -LRU_C, None, ALU.mult).then_inc(lam_ready, 1)

        with dve.Fori(1, ADA_FIRST // 2) as i:
            for parity in range(2):
                for k in range(DB):
                    add_first(i * 2 + parity, k, parity)
                    if k == 4:
                        finish_ada(i * 2 + (parity - 1), 1 - parity)
        finish_ada(ADA_FIRST - 1, 1)
        dve.wait_ge(mod_ready, 4)
        for c in range(CHUNKS):
            convert(0, 0, c)

        def modulated_gain(scale, name):
            own(dve.scalar_tensor_tensor(out=gain[:, :], in0=mod[:, scale * DB:(scale + 1) * DB], scalar=1.0,
                                         in1=col(name, 0, DB), op0=ALU.add, op1=ALU.mult))

        modulated_gain(1, "g_norm_mix")
        norm(0, 0, 0)

        def conv(q):
            for j in range(CONV):
                tap = CONV - 1 - j
                for b in range(2):
                    blk = 2 * q + b
                    src = xr_pad[:, blk, tap:tap + T]
                    w = col("w_conv", tap * LB + blk)
                    if j == 0:
                        ins = dve.tensor_scalar(xc[:, blk, :], src, w, col("b_conv", blk), ALU.mult, ALU.add)
                    else:
                        ins = dve.scalar_tensor_tensor(out=xc[:, blk, :], in0=src, scalar=w, in1=xc[:, blk, :],
                                                       op0=ALU.mult, op1=ALU.add)
                if j < CONV - 1:
                    own(ins)
            ins.then_inc(conv_ready, 1)

        def multiplier(half):
            r = slice(4 * half, 4 * half + 4)
            buf = val4[:, :, :]
            dve.wait_ge(decays, half + 1)
            own(dve.tensor_tensor(buf, gate_r[:, r, :], gate_r[:, r, :], ALU.mult))
            dve.scalar_tensor_tensor(out=lru_t[:, r, :].rearrange("p b t -> p (b t)"), in0=buf.rearrange("p b t -> p (b t)"),
                                     scalar=1.0, in1=lru_t[:, r, :].rearrange("p b t -> p (b t)"),
                                     op0=ALU.add, op1=ALU.mult).then_inc(mult_sq, 1)

        def input_gate(half):
            r = slice(4 * half, 4 * half + 4)
            own(dve.tensor_tensor(gate_i[:, r, :], gate_i[:, r, :], xc[:, r, :], ALU.mult))

        def recurrence(half):
            r = slice(4 * half, 4 * half + 4)
            dve.wait_ge(mult_ready, half + 1)
            own(dve.tensor_tensor(gate_i[:, r, :], gate_i[:, r, :], lru_t[:, r, :], ALU.mult))
            for blk in range(4 * half, 4 * half + 4):
                ins = dve.tensor_tensor_scan(out=xc[:, blk, :], data0=gate_r[:, blk, :], data1=gate_i[:, blk, :],
                                             initial=0.0, op0=ALU.mult, op1=ALU.add)
            own(ins)

        def gated(half):
            r = slice(4 * half, 4 * half + 4)
            dve.wait_ge(gelu_ready, 1)
            dve.tensor_tensor(xc[:, r, :], xc[:, r, :], gelu[:, r, :], ALU.mult).then_inc(y_full, 1)

        def y_low(half):
            r = slice(4 * half, 4 * half + 4)
            dve.wait_ge(y_hi, half + 1)
            dve.tensor_tensor(mid_s[:, r, 1, :], xc[:, r, :], mid_s[:, r, 0, :].bitcast(F32), ALU.subtract)\
               .then_inc(y_ready, 1)

        def windows(g):
            w = WINDOWS[g]
            bufs = (pool_a, pool_b)
            src, n = pool_x, 1
            for j in range(g + 1):
                dst = bufs[j % 2]
                own(dve.tensor_tensor(dst[:, :, WPAD:], src[:, :, WPAD:], src[:, :, WPAD - n:WPAD - n + T], ALU.add))
                src, n = dst, 2 * n
            head = src[:, :, WPAD:WPAD + w - 1]
            for b in range(2):
                ins = dve.tensor_tensor(val[:, g % 2, b, 0:w - 1], head[:, b, :], inv_n[:, 0:w - 1], ALU.mult)
            own(ins)
            own(dve.tensor_tensor(val[:, g % 2, :, 0:w - 1], val[:, g % 2, :, 0:w - 1],
                                  pool_x[:, :, WPAD:WPAD + w - 1], ALU.subtract))
            dve.scalar_tensor_tensor(out=val[:, g % 2, :, w - 1:T], in0=src[:, :, WPAD + w - 1:WPAD + T], scalar=1.0 / w,
                                     in1=pool_x[:, :, WPAD + w - 1:WPAD + T], op0=ALU.mult, op1=ALU.subtract)\
               .then_inc(pooled, 1)
            dve.wait_ge(pooled, g + 1)

        def pool_scaled(g):
            dve.wait_ge(pool_mm, g + 1)
            for b in range(2):
                ins = dve.tensor_scalar(val[:, g % 2, b, :], pm[2][:, b * T:(b + 1) * T], col("ls_pool", 2 * g + b),
                                        None, ALU.mult)
            ins.then_inc(pool_full, 1)

        def pool_low(g):
            dve.wait_ge(pool_hi, g + 1)
            dve.tensor_tensor(mid_s[:, LB + 2 * g:LB + 2 * g + 2, 1, :], val[:, g % 2, :, :],
                              mid_s[:, LB + 2 * g:LB + 2 * g + 2, 0, :].bitcast(F32), ALU.subtract).then_inc(pool_ready, 1)

        def first_mid(q):
            def mid(c):
                if c == 0:
                    finish_rides(S_IN + q)
                add_rides(S_IN + q, c)
                if c == 1 and q in (7, 8):
                    multiplier(q - 7)
                if c == 2 and q in (7, 8):
                    input_gate(q - 7)
                if c == 0 and q >= 10:
                    pool_scaled(q - 10)
                if c == 1 and q in (10, 11):
                    recurrence(q - 10)
                if c == 2 and q in (10, 11):
                    gated(q - 10)
                if c == 3 and q == 11:
                    y_low(0)
                if c == 3 and q >= 10:
                    pool_low(q - 10)
            return mid

        dve.wait_ge(constants, 22)
        own(dve.memset(pool_b[:, :, 0:WPAD], 0.0))
        for q in range(IN_SLABS):
            if q < 4:
                dst = xr_pad[:, 2 * q:2 * q + 2, PAD:]
            elif q < 8:
                dst = gelu[:, 2 * (q - 4):2 * (q - 4) + 2, :]
            else:
                dst = pool_x[:, :, WPAD:]
            turn(q // 2, q % 2, dst, mid=first_mid(q))
            if q < 4:
                conv(q)
            elif q >= 8:
                windows(q - 8)
        y_low(1)
        pool_scaled(2)
        pool_low(2)
        pool_scaled(3)
        pool_low(3)

        def residual_turn(S, k, gate, n_norm, pair, s, kt_next=KT, mid=None, last=False):
            def both(c):
                if c == 0 and k >= 1:
                    add_squares(n_norm, k - 1)
                if mid is not None:
                    mid(c)
            if last:
                both(0)
                evacuate(2 * pair + s + offset[0], s, val[:, s, :, :])
            else:
                turn(pair, s, val[:, s, :, :], mid=both, kt_next=kt_next)
            residual(S, gate, k, val[:, s]).then_inc(x_updated, 1)
            if k == OUT_SLABS - 1:
                add_squares(n_norm, k)

        def out_mid(q):
            def mid(c):
                if c == 0:
                    finish_rides(S_OUT + q)
                add_rides(S_OUT + q, c)
            return mid
        dve.wait_ge(mod_ready, 6)
        for q in range(OUT_SLABS):
            residual_turn(S_OUT + q, q, 2, 1, (S_OUT + q) // 2, q % 2, mid=out_mid(q))
        finish_rides(S_FFN)
        dve.wait_ge(mod_ready, 10)
        modulated_gain(4, "g_norm_ffn")
        norm(1, 1, 3)

        def conv_2(s, i):
            base = s * FB
            for j in range(CONV_2):
                tap = CONV_2 - 1 - j
                for b in range(2):
                    src = up_pad[:, s, b, tap:tap + T]
                    k = i * 2 + (base + b)
                    w = par[:, bass.ds(k + (PARAMS["conv_w_2"][0] + tap * 2 * FB), 1)]
                    dst = conv_o[:, s, b, :]
                    if j == 0:
                        bias = par[:, bass.ds(k + PARAMS["conv_b_2"][0], 1)]
                        ins = dve.tensor_scalar(dst, src, w, bias, ALU.mult, ALU.add)
                    else:
                        ins = dve.scalar_tensor_tensor(out=dst, in0=src, scalar=w, in1=dst, op0=ALU.mult, op1=ALU.add)
                if j < CONV_2 - 1:
                    own(ins)
            return ins

        def ffn(first, n_sq, gate):
            for g, gu, n, down, kt, pairs in groups(first):
                h0 = (first == S_FFN2) * (FB // 2) + pairs

                def hidden_pair(i, kt_next=KT, mid=None):
                    pair = i + gu // 2
                    h = i + h0
                    if first == S_FFN:
                        turn(pair, 0, val[:, 0, :, :], mid=mid and (lambda c: mid(2 * i, c)))
                        turn(pair, 1, val[:, 1, :, :], mid=mid and (lambda c: mid(2 * i + 1, c)), kt_next=kt_next)
                        a, b = val[:, 0, :, :], val[:, 1, :, :]
                    else:
                        turn(pair, 0, up_pad[:, 0, :, PAD_2:])
                        conv_2(0, i + pairs).then_inc(val_ready, 1)
                        turn(pair, 1, up_pad[:, 1, :, PAD_2:], kt_next=kt_next)
                        own(conv_2(1, i + pairs))
                        a, b = conv_o[:, 0, :, :], conv_o[:, 1, :, :]
                    dve.wait_ge(act_done, h + 1 + act_before)
                    hid = (lambda part: mid_s[:, 2 * i:2 * i + 2, part, :]) if isinstance(i, int) else \
                        (lambda part: mid_s[:, bass.ds(i * 2, 2), part, :])
                    dve.tensor_tensor(hid(0), a, b, ALU.mult)
                    own(dve.tensor_tensor(b, a, b, ALU.mult))
                    dve.tensor_tensor(hid(1), b, hid(0).bitcast(F32), ALU.subtract).then_inc(mid_ready, 1)

                act_before = 0 if first == S_FFN else 4 + 16
                done = 0
                if first == S_FFN and g == 0:
                    done = (len(RIDES) + 2 - S_FFN) // 2
                    for i in range(done):
                        def mid(slab, c):
                            if c == 0 and slab > 0:
                                finish_rides(S_FFN + slab)
                            add_rides(S_FFN + slab, c)
                        hidden_pair(i, mid=mid)
                    finish_rides(S_FFN + 2 * done)
                per = 1 if first == S_FFN else 2 * (CONV_2 - 1) + 2
                with dve.Fori(done, n - 1) as i:
                    steps.enter(i - done, per)
                    hidden_pair(i)
                steps.leave(n - 1 - done)
                hidden_pair(n - 1, kt)
                if g == 0 and gate is not None:
                    dve.wait_ge(mod_ready, ADA_PARTS)
                if g < len(FFN_GROUPS) - 1:
                    with dve.Fori(0, OUT_SLABS // 2) as i:
                        for s in range(2):
                            turn(i + down // 2, s, val[:, s, :, :])
                            for b in range(2):
                                k = i * 4 + (2 * s + b)
                                xs = x_t[:, bass.ds(k, 1), :].rearrange("p b t -> p (b t)")
                                if gate is None:
                                    dve.tensor_tensor(xs, xs, val[:, s, b, :], ALU.add)
                                else:
                                    dve.scalar_tensor_tensor(out=xs, in0=val[:, s, b, :],
                                                             scalar=mod[:, bass.ds(k + gate * DB, 1)],
                                                             in1=xs, op0=ALU.mult, op1=ALU.add)
                else:
                    for q in range(OUT_SLABS):
                        end = down + q + 1 == S_END
                        residual_turn(down + q, q, gate, n_sq, (down + q) // 2, q % 2,
                                      kt_next=kt if q < OUT_SLABS - 1 else KT, last=end)

        ffn(S_FFN, 2, 5)
        inv_rms(2)
        for q in range(OUT_SLABS):
            for b in range(2 * q, 2 * q + 2):
                ins = dve.scalar_tensor_tensor(out=x_t[:, b, :], in0=x_t[:, b, :], scalar=col("g_norm_final", b),
                                               in1=rstd[:, :], op0=ALU.mult, op1=ALU.mult)
            ins.then_inc(x_updated, 1)
            if q >= 1:
                add_squares(3, q - 1)
        add_squares(3, OUT_SLABS - 1)
        own(dve.tensor_copy(gain[:, :], col("attn_norm_w_2", 0, DB)))
        norm(3, 2, None)

        def rotate_m(j):
            dve.wait_ge(swapped, j + 1)
            xs = qk_m[0:ROT, 2 * (j % 4):2 * (j % 4) + 2, j // 4, :]
            cos = rope_m[:, 0:1, :].to_broadcast([ROT, 2, T])
            sin = rope_m[:, 1:2, :].to_broadcast([ROT, 2, T])
            t = val[0:ROT, 0, :, :]
            own(dve.tensor_tensor(t, pm[0][0:ROT, :].rearrange("p (b t) -> p b t", b=2), sin, ALU.mult))
            own(dve.tensor_tensor(xs, xs, cos, ALU.mult))
            dve.tensor_tensor(xs, xs, t, ALU.add).then_inc(rotated, 1)

        def rotate_r(h, which):
            xs = qk_r[:, h, which, :, :]
            cos = rope_r[:, 0:1, :].to_broadcast([P, 2, T])
            sin = rope_r[:, 1:2, :].to_broadcast([P, 2, T])
            dve.tensor_tensor(val[:, 0, :, :], xs, cos, ALU.mult)
            own(dve.tensor_tensor(val[:, 1, :, :], xs, sin, ALU.mult))
            dve.tensor_tensor(xs[:, 0, :], val[:, 0, 0, :], val[:, 1, 1, :], ALU.subtract)
            return dve.tensor_tensor(xs[:, 1, :], val[:, 0, 1, :], val[:, 1, 0, :], ALU.add)

        def moba_max(h):
            dve.wait_ge(scores_mm, h + 1)
            if h >= 2:
                dve.wait_ge(turned, h - 1)
            own(dve.tensor_tensor(prob[:, h % 2, :], pm[1][:, 0:3 * P], cmask[:, :], ALU.min))
            dve.tensor_reduce(s_max[:, 0:1], prob[:, h % 2, 0:P], AX.X, ALU.max)
            own(dve.tensor_reduce(s_max[:, 1:2], prob[:, h % 2, P:3 * P], AX.X, ALU.max))
            dve.tensor_scalar(s_neg[:, :], s_max[:, :], -(MOBA_DIM ** -0.5), None, ALU.mult).then_inc(maxed, 1)

        def moba_softmax(h):
            dve.wait_ge(exped, h + 1)
            own(dve.reciprocal(s_inv[:, :], s_sum[:, :]))
            dve.tensor_scalar(prob[:, h % 2, 0:P], prob[:, h % 2, 0:P], s_inv[:, 0:1], None, ALU.mult)
            dve.tensor_scalar(prob[:, h % 2, P:3 * P], prob[:, h % 2, P:3 * P], s_inv[:, 1:2], None, ALU.mult).then_inc(prob_ready, 1)

        def moba_low(h):
            dve.wait_ge(moba_hi, h + 1)
            dve.tensor_tensor(o_m[:, h, 1, :], pm[3][:, 0:T], o_m[:, h, 0, :].bitcast(F32), ALU.subtract)\
               .then_inc(moba_ready, 1)

        def ret_decay(h):
            dve.wait_ge(ret_scores, h + 1)
            if h == 0:
                dve.wait_ge(turned, MOBA_HEADS)
            else:
                dve.wait_ge(ret_mm, h)
            dve.tensor_tensor(prob[:, h % 2, 0:T], pm[0][:, 0:T], decay[:, h, :], ALU.mult)
            dve.tensor_tensor(prob[:, h % 2, T:3 * P], pm[0][:, T:3 * P], decay[:, h, 0:P], ALU.mult).then_inc(ret_decayed, 1)

        def ret_variance(h):
            dve.wait_ge(ret_summed, h + 1)
            dve.tensor_scalar(rstd[:, :], pm[2][:, 0:T], 1.0 / RET_DIM, EPS, ALU.mult, ALU.add).then_inc(ret_var, 1)

        def ret_inverse(h):
            dve.wait_ge(ret_std, h + 1)
            own(dve.reciprocal(rstd[:, :], rstd[:, :]))

        def ret_gate(h):
            dve.wait_ge(act_done, FB // 2 + h + 1)
            o = pm[1][:, :].rearrange("p (b t) -> p b t", b=2)
            own(dve.tensor_tensor(val[:, 0, :, :], o, rstd[:, :].unsqueeze(1).to_broadcast([P, 2, T]), ALU.mult))
            for b in range(2):
                ins = dve.scalar_tensor_tensor(out=val[:, 0, b, :], in0=val[:, 0, b, :], scalar=col("ret_norm_w_2", 2 * h + b),
                                               in1=g_r[:, 2 * h + b, :], op0=ALU.mult, op1=ALU.mult)
            ins.then_inc(ret_full, 1)

        def ret_low(h):
            dve.wait_ge(ret_hi, h + 1)
            dve.tensor_tensor(o_r[:, 2 * h:2 * h + 2, 1, :], val[:, 0, :, :],
                              o_r[:, 2 * h:2 * h + 2, 0, :].bitcast(F32), ALU.subtract).then_inc(ret_ready, 1)
            dve.wait_ge(ret_ready, h + 1)

        def second_mid(q):
            def mid(c):
                if c == 0 and 2 <= q <= 9:
                    rotate_m(q - 2)
                if c == 0 and 0 <= q - 13 < 8:
                    moba_max(q - 13)
                if c == 2 and 0 <= q - 13 < 8:
                    moba_softmax(q - 13)
                if c == 1 and 0 <= q - 16 < 8:
                    moba_low(q - 16)
                if 24 <= q <= 30 and q % 2 == 0 and c == 0:
                    ret_decay((q - 24) // 2)
                if 26 <= q <= 32 and q % 2 == 0:
                    h = (q - 26) // 2
                    if c == 0:
                        ret_variance(h)
                    if c == 1:
                        ret_inverse(h)
                    if c == 2:
                        ret_gate(h)
                    if c == 3:
                        ret_low(h)
            return mid

        for q in range(IN2_SLABS):
            if q < 8:
                dst = qk_m[:, 2 * (q % 4):2 * (q % 4) + 2, q // 4, :]
            elif q < 12:
                dst = v_m[:, :, SLAB * (q - 8):SLAB * (q - 7)]
            elif q < 20:
                dst = qk_r[:, (q - 12) % 4, (q - 12) // 4, :, :]
            elif q < 24:
                dst = v_r[:, :, SLAB * (q - 20):SLAB * (q - 19)]
            elif q < 28:
                dst = g_r[:, 2 * (q - 24):2 * (q - 24) + 2, :]
            else:
                dst = val[:, q % 2, :, :]
            if q >= 30:
                dve.wait_ge(act_done, FB // 2 + 4 + q - 29)
            turn((S_IN2 + q) // 2, q % 2, dst, mid=second_mid(q))
            if 12 <= q < 20:
                rotate_r((q - 12) % 4, (q - 12) // 4).then_inc(qkv_stored, 1)
            elif q < 28:
                dve.nop().then_inc(qkv_stored, 1)

        for m in range(OUT_SLABS):
            pair, s = (S_MERGE + m) // 2, m % 2
            for c in range(CHUNKS):
                if s == 0:
                    convert(pair, 1, c)
                else:
                    convert(pair + 1, 0, c)
                if c == 1:
                    if m == 0:
                        dve.wait_ge(act_done, FB // 2 + 4 + 16)
                    if m >= 1:
                        dve.wait_ge(merged_ready, m)
                    evacuate(S_MERGE + 2 * m, 0, val[:, 0, :, :])
                    own(dve.tensor_tensor(val[:, 0, :, :], val[:, 0, :, :], sig_r[:, 2 * m:2 * m + 2, :], ALU.mult))
            evacuate(S_MERGE + 2 * m + 1, 1, val[:, 1, :, :])
            own(dve.tensor_tensor(val[:, 1, :, :], val[:, 1, :, :], sig_m[:, 2 * m:2 * m + 2, :], ALU.mult))
            dve.tensor_tensor(val[:, 0, :, :], val[:, 0, :, :], val[:, 1, :, :], ALU.add).then_inc(merged_t, 1)
            dve.wait_ge(merged_hi, m + 1)
            dve.tensor_tensor(h_s[:, 2 * m:2 * m + 2, 1, :], val[:, 0, :, :],
                              h_s[:, 2 * m:2 * m + 2, 0, :].bitcast(F32), ALU.subtract).then_inc(merged_ready, 1)
        offset[0] = OUT_SLABS
        dve.wait_ge(merged_ready, OUT_SLABS)
        for q in range(OUT_SLABS):
            residual_turn(S_OUT2 + q, q, None, 4, (S_OUT2 + q) // 2, q % 2)
        own(dve.tensor_copy(gain[:, :], col("ffn_norm_w_2", 0, DB)))
        norm(4, 3, None)
        own(dve.memset(up_pad[:, :, :, 0:PAD_2], 0.0))
        ffn(S_FFN2, 5, None)
        inv_rms(5)
        for b in range(DB):
            dve.scalar_tensor_tensor(out=out_t[:, b, :], in0=x_t[:, b, :], scalar=col("final_norm_w_2", b),
                                     in1=rstd[:, :], op0=ALU.mult, op1=ALU.mult).then_inc(out_ready, 1)

    ctx.close()


def chunked(w, kt=KT, order=None):
    k, n = w.shape
    a = w.reshape(k // (kt * P), kt, P, n // SLAB, SLAB).transpose(3, 0, 2, 1, 4)
    if order is not None:
        a = a[order]
    return np.ascontiguousarray(a).reshape(n // SLAB, k // (kt * P), P, kt * SLAB)


def tables():
    f = np.float32
    pos = np.arange(T, dtype=f)

    def angles(dim, theta):
        inv = f(theta) ** (-np.arange(0, dim, 2, dtype=f) / f(dim))
        return (pos[None, :] * inv[:, None].astype(f)).astype(np.float64)

    a = angles(RET_DIM, RET_THETA)
    rope_r = np.stack([np.cos(a), np.sin(a)], axis=1).astype(f)
    a = angles(ROT, MOBA_THETA)
    rope_m = np.stack([np.concatenate([np.cos(a), np.cos(a)]), np.concatenate([-np.sin(a), np.sin(a)])], axis=1).astype(f)
    log_g = np.log1p(-np.exp2(-5.0 - np.arange(RET_HEADS)))
    diff = np.arange(T)[None, :] - np.arange(P)[:, None]
    decay = np.where(diff[:, None, :] >= 0, np.exp(log_g[None, :, None] * np.maximum(diff, 0)[:, None, :]), 0.0)
    decay = (decay * RET_DIM ** -0.5).astype(f)
    causal = np.where(np.arange(P)[None, :] <= np.arange(P)[:, None], BIG, -BIG)
    cmask = np.concatenate([causal, np.full((P, P), BIG), causal], axis=1).astype(f)
    perm = np.roll(np.eye(ROT, dtype=f), ROT // 2, axis=1)
    return {"rope_r": rope_r, "rope_m": rope_m, "decay": decay, "cmask": cmask, "perm": perm,
            "ident": np.eye(P, dtype=f)}


def laid_out(inputs):
    a = {k: np.asarray(v) for k, v in inputs.items()}
    d = tables()
    d["x_fm"] = np.ascontiguousarray(a["x"][0].T)
    rows = [a[name].reshape(-1, P) for name in PARAMS]
    d["params"] = np.ascontiguousarray(np.concatenate(rows, axis=0).T)
    d["w_ada"] = a["w_ada"][0]
    d["w_in"] = chunked(a["w_in"][0])
    d["w_out"] = chunked(a["w_out"][0])
    d["w_rg_a"] = np.ascontiguousarray(a["w_rg_a"][0].reshape(LB, 2, LRU_HEAD, LRU_HEAD).transpose(1, 0, 2, 3))
    d["w_rg_i"] = np.ascontiguousarray(a["w_rg_i"][0].reshape(LB, 2, LRU_HEAD, LRU_HEAD).transpose(1, 0, 2, 3))
    d["w_pool"] = a["w_pool"][0]
    d["w_ffn_gate"] = chunked(a["w_ffn_gate"][0])
    d["w_ffn_up"] = chunked(a["w_ffn_up"][0])
    d["w_in_2"] = chunked(a["w_in_2"][0], order=IN2_ORDER)
    d["w_ret_up_2"] = chunked(a["w_ret_up_2"][0])
    d["w_moba_up_2"] = chunked(a["w_moba_up_2"][0])
    d["w_out_2"] = chunked(a["w_out_2"][0])
    d["w_ffn_a_2"] = chunked(a["w_ffn_up_2"][0][:, :D_FF])
    d["w_ffn_b_2"] = chunked(a["w_ffn_up_2"][0][:, D_FF:])
    for name in ("w_ffn_down", "w_ffn_down_2"):
        at = 0
        for g, n in enumerate(FFN_GROUPS):
            d[f"{name}{g}"] = chunked(a[name][0][at:at + n * SLAB], kt=2 * n // CHUNKS)
            at += n * SLAB
    return d


def kernel(**inputs):
    import concourse.bacc as _bacc
    from concourse.bass_utils import run_bass_kernel_spmd as _run

    nc = _bacc.Bacc("TRN2", target_bir_lowering=False, num_devices=1)
    arrays = {f"in_{k}": np.ascontiguousarray(v) for k, v in laid_out(inputs).items()}
    dram = {k[3:]: nc.dram_tensor(k, v.shape, F32, kind="ExternalInput").ap() for k, v in arrays.items()}
    out = nc.dram_tensor("out_fm", (D, T), F32, kind="ExternalOutput").ap()
    build(nc, dram, out)
    r = _run(nc, [arrays], core_ids=[0])
    return np.ascontiguousarray(np.asarray(r.results[0]["out_fm"]).T)[None]
```

```python
from contextlib import ExitStack

import concourse.bass as bass
import concourse.mybir as mybir
import numpy as np

F32 = mybir.dt.float32
F32R = mybir.dt.float32r
ACT = mybir.ActivationFunctionType
ALU = mybir.AluOpType
AX = mybir.AxisListType

P = 128
T = 256
D = 2048
DB = D // P
SLAB = 256
CHUNKS = 4
KT = DB // CHUNKS
RAW = 8
RING = 4
EPS = 1e-6

D_LRU = D // 2
LRU_HEAD = 64
LB = D_LRU // P
CONV = 4
LRU_C = 8.0
WINDOWS = (2, 4, 8, 16)
D_FF = 5632
FB = D_FF // P
N_MOD = 6
FFN_GROUPS = (8, 8, 6)

RET_HEADS, RET_DIM, RET_THETA = 4, 256, 10000.0
MOBA_HEADS, MOBA_DIM, MOBA_THETA = 8, 128, 500000.0
ROT = MOBA_DIM // 4
CONV_2 = 3
BIG = 3.0e38

IN_SLABS = (2 * D_LRU + D_LRU) // SLAB
OUT_SLABS = D // SLAB
IN2_SLABS = (4 * 1024 + 3 * 1024 + 2 * D) // SLAB

ADA_COLS = 1024
ADA_PARTS = N_MOD * D // ADA_COLS
ADA_FIRST = 4
ADA_RING = 8
RIDE_RING = 5

def _rides():
    at = {S: ([0, 1, 2, 3], []) for S in range(5)}
    at.update({5: ([0, 1, 2, 3], [3]), 6: ([0, 1, 2, 3], [1, 2, 3])})
    for S in range(7, 19):
        at[S] = ([0, 1, 2, 3], [3] if (S - 7) % 3 < 2 else [2, 3])
    for S in range(20, 30):
        at[S] = ([0, 1, 2] if S % 5 < 4 else [0, 1, 2, 3], [])
    return [(S, c, engine) for S, chunks in sorted(at.items()) for c in range(CHUNKS)
            for engine, mine in zip(("vector", "tensor"), chunks) if c in mine]


RIDE_AT = _rides()
RIDE_SLABS = RIDE_AT[-1][0] + 1
RIDE_PARTS = range(ADA_FIRST, ADA_PARTS)
assert len(RIDE_AT) == len(RIDE_PARTS) * DB


def _pieces(part, engine=None):
    first = (part - ADA_FIRST) * DB
    return [p for p in range(first, first + DB) if engine in (None, RIDE_AT[p][2])]


TURN_AT = {part: max(RIDE_AT[_pieces(part)[-1]][0] + 1, 5) for part in RIDE_PARTS}


def _counts():
    done = {"vector": ADA_FIRST * DB, "tensor": 0}
    piece_count, part_count = {}, {}
    for piece, (_, _, engine) in enumerate(RIDE_AT):
        done[engine] += 1
        piece_count[piece] = done[engine]
        part_count[ADA_FIRST + piece // DB] = done["vector"]
    return piece_count, part_count


PIECE_COUNT, PART_COUNT = _counts()

IN_ORDER = [*range(0, 4), *range(8, 12), *range(4, 8)]
IN2_ORDER = [*range(16, 28), *range(0, 16), *range(28, 44)]
V_SLABS = [*range(8, 12), *range(20, 24)]

PARAMS = {}
_at = 0
for _name, _rows in (
    ("c", DB), ("b_ada", N_MOD * DB), ("g_norm_mix", DB), ("w_conv", CONV * LB), ("b_conv", LB), ("b_rg_a", LB),
    ("b_rg_i", LB), ("lru_lambda", LB), ("ls_pool", LB), ("g_norm_ffn", DB), ("g_norm_final", DB),
    ("attn_norm_w_2", DB), ("ret_norm_w_2", LB), ("ffn_norm_w_2", DB), ("conv_w_2", CONV_2 * 2 * FB),
    ("conv_b_2", 2 * FB), ("final_norm_w_2", DB),
):
    PARAMS[_name] = (_at, _rows)
    _at += _rows
N_PARAMS = _at


class Steps:

    def __init__(self):
        self.base, self.done = 0, 0

    def next(self):
        self.done += 1
        return self.base + self.done

    def enter(self, i, per):
        self.outer, self.per = self.base + self.done, per
        self.base, self.done = self.outer + i * per, 0

    def leave(self, turns):
        assert self.done == self.per, (self.done, self.per)
        self.base, self.done = self.outer + turns * self.per, 0


def build(nc, dram, out):
    ctx = ExitStack()

    def at(name, shape, offset, dt=F32):
        return nc.alloc_sbuf_tensor_at(name, shape, dt, offset=offset)

    top = 16512
    def place(size):
        nonlocal top
        where, top = top, top + size
        return where

    raw = at("raw", [P, RAW, KT, SLAB], place(RAW * KT * SLAB * 4))
    split = at("split", [P, RING, KT, 2, SLAB], place(RING * KT * 2 * SLAB * 4), F32R)
    H_AT = place(DB * 2 * T * 4)
    h_s = at("h_s", [P, DB, 2, T], H_AT, F32R)
    MID = place(DB * 2 * T * 4)
    x_t = at("x_t", [P, DB, T], place(DB * T * 4))
    low = at("low", [P, 2, 2, T], place(2 * 2 * T * 4))
    val_at = place(2 * 2 * T * 4)
    val = at("val", [P, 2, 2, T], val_at)
    val4 = at("val4", [P, 4, T], val_at)
    par = at("par", [P, N_PARAMS], place(N_PARAMS * 4))
    mod = at("mod", [P, N_MOD * DB], place(N_MOD * DB * 4))
    ident = at("ident", [P, P], place(P * 4))
    ones = at("ones", [P, P], place(P * 4))
    gain = at("gain", [P, DB], place(DB * 4))
    c_act = at("c_act", [P, DB], place(DB * 4))
    lam_e = at("lam_e", [P, LB], place(32))
    lam_z = at("lam_z", [P, LB], place(32))
    lam_q = at("lam_q", [P, LB], place(32))
    lam_p = at("lam_p", [P, LB], place(32))
    lam_8 = at("lam_8", [P, LB], place(32))
    lam_n8 = at("lam_n8", [P, LB], place(32))
    inv_n = at("inv_n", [P, 16], place(64))
    s_max = at("s_max", [P, 2], place(32))
    s_neg = at("s_neg", [P, 2], place(32))
    s_sum = at("s_sum", [P, 2], place(32))
    s_inv = at("s_inv", [P, 2], place(32))
    SSQ = place(2048)
    ssq = at("ssq", [P, 2, T], SSQ)
    RSTD = place(1024)
    rstd = at("rstd", [P, T], RSTD)
    F = place(0)

    mid_s = at("mid_s", [P, DB, 2, T], MID, F32R)
    rg_a = at("rg_a", [P, LB, P], MID)
    rg_i = at("rg_i", [P, LB, P], MID + 4096)
    a_sq = at("a_sq", [P, LB // 2, T], MID + 4096)
    gate_r = at("gate_r", [P, LB, T], MID + 16384)
    gate_i = at("gate_i", [P, LB, T], MID + 24576)
    qk_r = at("qk_r", [P, RET_HEADS, 2, 2, T], MID)
    o_r = at("o_r", [P, LB, 2, T], MID, F32R)
    v_r = at("v_r", [P, 2, 1024], MID + 16384)
    g_r = at("g_r", [P, LB, T], MID + 24576)
    sig_m = at("sig_m", [P, DB, T], MID + 16384)

    acc = at("acc", [P, 2, ADA_COLS], F)
    ride = at("ride", [P, RIDE_RING, ADA_COLS], F + 8192)
    ada = at("ada", [P, ADA_RING, ADA_COLS], H_AT)
    w_pool = at("w_pool_sb", [P, 4, 2, 256], MID + 8192)
    PAD = CONV - 1
    xr_pad = at("xr_pad", [P, LB, PAD + T], F + 28672)
    lru_t = at("lru_t", [P, LB, T], F + 28672)
    xc = at("xc", [P, LB, T], F + 36960)
    WPAD = 16
    pool_x = at("pool_x", [P, 2, WPAD + T], F + 45152)
    pool_a = at("pool_a", [P, 2, WPAD + T], F + 45152 + 2176)
    pool_b = at("pool_b", [P, 2, WPAD + T], SSQ)

    qk_m = at("qk_m", [P, MOBA_HEADS, 2, T], F)
    o_m = at("o_m", [P, MOBA_HEADS, 2, T], F, F32R)
    v_m = at("v_m", [P, 2, 1024], F + 16384)
    sig_r = at("sig_r", [P, DB, T], F + 16384)
    rope_r = at("rope_r", [P, 2, T], F + 32768)
    rope_m = at("rope_m", [ROT, 2, T], F + 34816)
    decay = at("decay", [P, RET_HEADS, T], F + 36864)
    cmask = at("cmask", [P, 3 * P], F + 40960)
    prob = at("prob", [P, 2, 3 * P], F + 42496)
    prob_t = at("prob_t", [P, 3 * P], F + 45568)
    perm = at("perm", [ROT, ROT], F + 47104)
    PAD_2 = CONV_2 - 1
    sq_gf = at("sq_gf", [P, 2, 2, T], F + 16384)
    ssq_gf = at("ssq_gf", [P, 2, T], F + 20480)
    rstd_h = at("rstd_h", [P, T], F + 47360)
    rstd_col = at("rstd_col", [P, 2], F + 48384)
    up_pad = at("up_pad", [P, 2, 2, PAD_2 + T], F)
    conv_o = at("conv_o", [P, 2, 2, T], F + 4352)
    out_t = at("out_t", [P, DB, T], MID)
    assert F + 49504 <= nc.sbuf_usable_end, (F + 49504, nc.sbuf_usable_end)

    def col(name, k=0, n=1):
        a = PARAMS[name][0] + k
        return par[:, a:a + n]

    ps = ctx.enter_context(nc.psum_tensor("ps", [P, 2, 2, 512], F32))
    pm = [ctx.enter_context(nc.psum_tensor(f"pm{k}", [P, 512], F32)) for k in range(4)]

    def sem(name):
        return ctx.enter_context(nc.semaphore(name))

    raw_loaded = [sem(f"raw_loaded{k}") for k in range(RAW)]
    hi_ready = sem("hi_ready")
    lo_ready = sem("lo_ready")
    chunk_used = sem("chunk_used")
    low_copied = sem("low_copied")
    evacuated = sem("evacuated")
    params_loaded = sem("params_loaded")
    x_loaded = sem("x_loaded")
    side_loaded = sem("side_loaded")
    tables_loaded = sem("tables_loaded")
    ident_loaded = sem("ident_loaded")
    constants = sem("constants")
    ada_loaded = [sem(f"ada_loaded{k}") for k in range(ADA_RING)]
    ride_loaded = [sem(f"ride_loaded{k}") for k in range(RIDE_RING)]
    c_ready = sem("c_ready")
    ada_added = sem("ada_added")
    ada_multiplied = sem("ada_multiplied")
    ada_turned = sem("ada_turned")
    row_copied = sem("row_copied")
    row_turned = sem("row_turned")
    mod_ready = sem("mod_ready")
    squared = sem("squared")
    x_updated = sem("x_updated")
    ssq_added = sem("ssq_added")
    gf_squared = sem("gf_squared")
    gf_added = sem("gf_added")
    rstd_ready = sem("rstd_ready")
    rstd_turned = sem("rstd_turned")
    ssq_summed = sem("ssq_summed")
    var_ready = sem("var_ready")
    std_ready = sem("std_ready")
    norm_t = sem("norm_t")
    norm_hi = sem("norm_hi")
    h_ready = sem("h_ready")
    lam_exp = sem("lam_exp")
    lam_abs = sem("lam_abs")
    lam_ready = sem("lam_ready")
    conv_ready = sem("conv_ready")
    gates_mm = sem("gates_mm")
    gates_read = sem("gates_read")
    decays = sem("decays")
    mult_sq = sem("mult_sq")
    mult_ready = sem("mult_ready")
    gelu_ready = sem("gelu_ready")
    y_full = sem("y_full")
    y_hi = sem("y_hi")
    y_ready = sem("y_ready")
    pooled = sem("pooled")
    pool_mm = sem("pool_mm")
    pool_hi = sem("pool_hi")
    pool_ready = sem("pool_ready")
    val_ready = sem("val_ready")
    act_done = sem("act_done")
    mid_ready = sem("mid_ready")
    qkv_stored = sem("qkv_stored")
    swapped = sem("swapped")
    rotated = sem("rotated")
    scores_mm = sem("scores_mm")
    maxed = sem("maxed")
    exped = sem("exped")
    prob_ready = sem("prob_ready")
    turned = sem("turned")
    prob_copied = sem("prob_copied")
    moba_mm = sem("moba_mm")
    moba_hi = sem("moba_hi")
    moba_ready = sem("moba_ready")
    ret_scores = sem("ret_scores")
    ret_decayed = sem("ret_decayed")
    ret_mm = sem("ret_mm")
    ret_squared = sem("ret_squared")
    ret_summed = sem("ret_summed")
    ret_var = sem("ret_var")
    ret_std = sem("ret_std")
    ret_full = sem("ret_full")
    ret_hi = sem("ret_hi")
    ret_ready = sem("ret_ready")
    merged_t = sem("merged_t")
    merged_hi = sem("merged_hi")
    merged_ready = sem("merged_ready")
    out_ready = sem("out_ready")
    stored = sem("stored")
    dve_step = sem("dve_step")

    S_IN = 0
    S_OUT = S_IN + IN_SLABS
    S_FFN = S_OUT + OUT_SLABS
    FFN_SPAN = sum(2 * n + OUT_SLABS for n in FFN_GROUPS)
    S_IN2 = S_FFN + FFN_SPAN
    S_MERGE = S_IN2 + IN2_SLABS
    S_OUT2 = S_MERGE + OUT_SLABS
    S_FFN2 = S_OUT2 + OUT_SLABS
    S_END = S_FFN2 + FFN_SPAN

    def groups(first):
        S, pairs = first, 0
        for g, n in enumerate(FFN_GROUPS):
            yield g, S, n, S + 2 * n, 2 * n // CHUNKS, pairs
            S += 2 * n + OUT_SLABS
            pairs += n

    def tiles_of(S):
        for first in (S_FFN, S_FFN2):
            for _, _, _, down, kt, _ in groups(first):
                if down <= S < down + OUT_SLABS:
                    return kt
        return KT

    block = ctx.enter_context(nc.Block())

    @block.sync
    def _(sp):
        sp.dma_start(par[:, :], dram["params"]).then_inc(params_loaded, 16)

        def load(pair, c, src, kt=KT):
            if not (isinstance(pair, int) and pair == 0):
                sp.wait_ge(lo_ready, 2 * CHUNKS * pair + c - RAW + 1)
            sp.dma_start(raw[:, c, 0:kt, :].rearrange("p k n -> p (k n)"), src).then_inc(raw_loaded[c], 16)

        def chunk(w, slab, c):
            return w[bass.ds(slab, 1), c].rearrange("a p n -> p (a n)")

        sp.dma_start(x_t[:, :, :], dram["x_fm"].rearrange("(b p) t -> p b t", p=P)).then_inc(x_loaded, 16)
        for part in range(ADA_FIRST):
            for k in range(DB):
                if part * DB + k >= ADA_RING:
                    sp.wait_ge(ada_added, part * DB + k - ADA_RING + 1)
                sp.dma_start(ada[:, k % ADA_RING, :], dram["w_ada"][k * P:(k + 1) * P, part * ADA_COLS:(part + 1) * ADA_COLS])\
                  .then_inc(ada_loaded[k % ADA_RING], 16)
        for c in range(2 * CHUNKS):
            load(0, c, dram["w_in"][c // CHUNKS, c % CHUNKS])

        done_pairs = -(-(RIDE_SLABS * CHUNKS + RAW) // (2 * CHUNKS))
        for G in range(RAW, done_pairs * 2 * CHUNKS):
            for piece, (S, c, _) in enumerate(RIDE_AT):
                if CHUNKS * S + c == G - RAW:
                    part, k, last = ADA_FIRST + piece // DB, piece % DB, piece - RIDE_RING
                    if last >= 0:
                        sp.wait_ge(ada_added if RIDE_AT[last][2] == "vector" else ada_multiplied, PIECE_COUNT[last])
                    sp.dma_start(ride[:, piece % RIDE_RING, :],
                                 dram["w_ada_late"][k * P:(k + 1) * P, part - ADA_FIRST])\
                      .then_inc(ride_loaded[piece % RIDE_RING], 16)
            S, c = G // CHUNKS, G % CHUNKS
            if S < S_OUT:
                src = dram["w_in"][S, c]
            elif S < S_FFN:
                src = dram["w_out"][S - S_OUT, c]
            else:
                src = (dram["w_ffn_gate"], dram["w_ffn_up"])[S % 2][(S - S_FFN) // 2, c]
            load(S // 2, CHUNKS * (S % 2) + c, src)

        def stream_ffn(wa, wb, wd, first, done):
            for g, gu, n, down, kt, pairs in groups(first):
                with sp.Fori(done if g == 0 else 0, n) as i:
                    for c in range(2 * CHUNKS):
                        load(i + gu // 2, c, chunk((wa, wb)[c // CHUNKS], i + pairs, c % CHUNKS))
                with sp.Fori(0, OUT_SLABS // 2) as i:
                    for c in range(2 * CHUNKS):
                        load(i + down // 2, c, chunk(wd[g], i * 2 + c // CHUNKS, c % CHUNKS), kt)

        stream_ffn(dram["w_ffn_gate"], dram["w_ffn_up"], [dram[f"w_ffn_down{g}"] for g in range(3)], S_FFN,
                   done_pairs - S_FFN // 2)
        with sp.Fori(0, IN2_SLABS // 2) as i:
            for c in range(2 * CHUNKS):
                load(i + S_IN2 // 2, c, chunk(dram["w_in_2"], i * 2 + c // CHUNKS, c % CHUNKS))
        with sp.Fori(0, OUT_SLABS // 2) as i:
            for c in range(2 * CHUNKS):
                w = (dram["w_ret_up_2"], dram["w_moba_up_2"])[c // 2 % 2]
                load(i + S_MERGE // 2, c, chunk(w, i * 2 + c // CHUNKS, c % 2))
        with sp.Fori(0, OUT_SLABS // 2) as i:
            for c in range(2 * CHUNKS):
                load(i + S_OUT2 // 2, c, chunk(dram["w_out_2"], i * 2 + c // CHUNKS, c % CHUNKS))
        stream_ffn(dram["w_ffn_a_2"], dram["w_ffn_b_2"], [dram[f"w_ffn_down_2{g}"] for g in range(3)], S_FFN2, 0)

        for j in range(4):
            sp.wait_ge(out_ready, j + 1)
            sp.dma_start(out.rearrange("(b p) t -> p b t", p=P)[:, 4 * j:4 * j + 4, :], out_t[:, 4 * j:4 * j + 4, :])\
              .then_inc(stored, 16)
        sp.wait_ge(stored, 64)

    @block.gpsimd
    def _(pool):
        pool.memset(ones[:, :], 1.0).then_inc(constants, 1)
        pool.memset(rg_a[:, :, :], 0.0).then_inc(constants, 1)
        pool.memset(rg_i[:, :, :], 0.0).then_inc(constants, 1)
        pool.memset(xr_pad[:, :, 0:PAD], 0.0).then_inc(constants, 1)
        pool.memset(pool_x[:, :, 0:WPAD], 0.0).then_inc(constants, 1)
        pool.memset(pool_a[:, :, 0:WPAD], 0.0).then_inc(constants, 1)
        for n in range(16):
            pool.memset(inv_n[:, n:n + 1], 1.0 / (n + 1)).then_inc(constants, 1)
        pool.dma_start(ident[:, :], dram["ident"]).then_inc(ident_loaded, 16)
        pool.dma_start(w_pool[:, :, :, :], dram["w_pool"].rearrange("g (k p) n -> p g k n", p=P)).then_inc(side_loaded, 16)
        pool.wait_ge(constants, 3)
        for w, sb in ((dram["w_rg_a"], rg_a), (dram["w_rg_i"], rg_i)):
            for k in range(2):
                pool.dma_start(sb[64 * k:64 * k + 64, :, 64 * k:64 * k + 64], w[k].rearrange("h i j -> i h j"))\
                    .then_inc(side_loaded, 16)
        pool.wait_ge(chunk_used, CHUNKS * S_FFN)
        pool.dma_start(rope_r[:, :, :], dram["rope_r"]).then_inc(tables_loaded, 16)
        pool.dma_start(rope_m[:, :, :], dram["rope_m"]).then_inc(tables_loaded, 16)
        pool.dma_start(decay[:, :, :], dram["decay"]).then_inc(tables_loaded, 16)
        pool.dma_start(cmask[:, :], dram["cmask"]).then_inc(tables_loaded, 16)
        pool.dma_start(perm[:, :], dram["perm"]).then_inc(tables_loaded, 16)

    @block.tensor
    def _(pe):
        def slab(S, s, acts, kt=KT, guard=None, tok=False, rides=False, after=None):
            if not (isinstance(S, int) and S < 2):
                pe.wait_ge(evacuated, evac_count_of(S) - 1)
            for c in range(CHUNKS):
                if guard is not None:
                    guard(c)
                multiply(CHUNKS * S + c, c, s, acts, c * kt, kt, c == 0, c == CHUNKS - 1, tok)
                if rides:
                    multiply_rides(S, c)
                if after is not None:
                    after(c)

        def multiply(G, slot, s, acts, k0, kt, first, last, tok=False):
            pe.wait_ge(lo_ready, G + 1)
            for k in range(kt):
                start, stop = first and k == 0, last and k == kt - 1
                for b in range(2):
                    if tok:
                        pe.matmul(ps[:, s, b, :], acts[:, k0 + k, 0, b * P:(b + 1) * P],
                                  split[:, slot, k, :, :].rearrange("p h n -> p (h n)"), start=start, stop=False)
                        mm = pe.matmul(ps[:, s, b, 0:SLAB], acts[:, k0 + k, 1, b * P:(b + 1) * P],
                                       split[:, slot, k, 0, :], start=False, stop=stop)
                    else:
                        pe.matmul(ps[:, s, b, :], split[:, slot, k, 0, b * P:(b + 1) * P],
                                  acts[:, k0 + k, :, :].rearrange("p h t -> p (h t)"), start=start, stop=False)
                        mm = pe.matmul(ps[:, s, b, 0:T], split[:, slot, k, 1, b * P:(b + 1) * P],
                                       acts[:, k0 + k, 0, :], start=False, stop=stop)
            mm.then_inc(chunk_used, 1)

        offset = [0]

        def evac_count_of(S):
            return S + offset[0]

        def turn_ada(part, parity, added):
            pe.wait_ge(ada_added, added)
            for j in range(8):
                mm = pe.matmul(pm[3][:, 8 * parity + j:8 * parity + j + 1], acc[:, parity, j * P:(j + 1) * P],
                               ones[:, 0:1], start=True, stop=True)
            mm.then_inc(ada_turned, 1)

        def row_free(part):
            if part == ADA_FIRST:
                pe.wait_ge(gates_read, 4)
            else:
                pe.wait_ge(row_copied, part - ADA_FIRST)

        def multiply_rides(S, c):
            for piece, at in enumerate(RIDE_AT):
                if at == (S, c, "tensor"):
                    part, slot = ADA_FIRST + piece // DB, piece % RIDE_RING
                    first = piece == _pieces(part, "tensor")[0]
                    if first:
                        row_free(part)
                    pe.wait_ge(ride_loaded[slot], 16 * (piece // RIDE_RING + 1))
                    for j in range(2):
                        mm = pe.matmul(pm[j][0:1, :], c_act[:, piece % DB:piece % DB + 1], ride[:, slot, j * 512:(j + 1) * 512],
                                       start=first, stop=False)
                    mm.then_inc(ada_multiplied, 1)
            for part in RIDE_PARTS:
                if (TURN_AT[part], 1) == (S, c):
                    if not _pieces(part, "tensor"):
                        row_free(part)
                    pe.wait_ge(ada_added, PART_COUNT[part])
                    for j in range(2):
                        mm = pe.matmul(pm[j][0:1, :], ones[:, 0:1], acc[:, part % 2, j * 512:(j + 1) * 512],
                                       start=not _pieces(part, "tensor"), stop=True)
                    mm.then_inc(ada_turned, 1)

        def sum_squares(n):
            pe.wait_ge(ssq_added, OUT_SLABS * (n + 1))
            if n == 2:
                pe.wait_ge(gf_added, OUT_SLABS)
                pe.matmul(pm[2][:, T:2 * T], ones[:, :], ssq_gf[:, 0, :], start=True, stop=False)
                pe.matmul(pm[2][:, T:2 * T], ones[:, :], ssq_gf[:, 1, :], start=False, stop=True)
            pe.matmul(pm[2][:, 0:T], ones[:, :], ssq[:, 0, :], start=True, stop=False)
            pe.matmul(pm[2][:, 0:T], ones[:, :], ssq[:, 1, :], start=False, stop=True).then_inc(ssq_summed, 1)

        def normed(k, n=None):
            def guard(c):
                if n is not None and c == 2:
                    sum_squares(n)
                pe.wait_ge(h_ready, DB * k + KT * (c + 1))
            return guard

        pe.wait_ge(constants, 1)
        pe.wait_ge(c_ready, 1)
        for part in range(ADA_FIRST):
            if part == 0:
                sum_squares(0)
            if part >= 2:
                pe.wait_ge(mod_ready, part - 1)
            turn_ada(part, part % 2, (part + 1) * DB)

        def gates(q):
            pe.wait_ge(conv_ready, q + 1)
            if q == 0:
                pe.wait_ge(side_loaded, 16 * 5)
            if q >= 1:
                pe.wait_ge(gates_read, q)
            for b in range(2):
                blk = 2 * q + b
                pe.matmul(pm[b][:, 0:T], rg_a[:, blk, :], xc[:, blk, :], start=True, stop=True)
                mm = pe.matmul(pm[b][:, T:2 * T], rg_i[:, blk, :], xc[:, blk, :], start=True, stop=True)
            mm.then_inc(gates_mm, 1)

        def pool_product(g):
            pe.wait_ge(pooled, g + 1)
            if g >= 1:
                pe.wait_ge(pool_ready, g)
            for b in range(2):
                for k in range(2):
                    mm = pe.matmul(pm[2][:, b * T:(b + 1) * T], w_pool[:, g, k, b * P:(b + 1) * P],
                                   val[:, g % 2, k, :], start=(k == 0), stop=(k == 1))
            mm.then_inc(pool_mm, 1)

        for q in range(IN_SLABS):
            slab(S_IN + q, q % 2, h_s, guard=normed(0) if q == 0 else None, rides=True)
            if 1 <= q <= 4:
                gates(q - 1)
            if 5 <= q <= 8:
                pool_product(q - 5)

        def mixed(c):
            pe.wait_ge(pool_ready if c < 2 else y_ready, 2 * (c % 2 + 1))
        for q in range(OUT_SLABS):
            slab(S_OUT + q, q % 2, mid_s, guard=mixed if q == 0 else None, rides=True)
        sum_squares(1)

        def ffn(first, k_h, n_sq, h_s, mid_s, n_in=None):
            for g, gu, n, down, kt, pairs in groups(first):
                done = 0
                if g == 0:
                    done = (RIDE_SLABS + 2 - S_FFN) // 2 if first == S_FFN else 1
                    for i in range(done):
                        for s in range(2):
                            slab(gu + 2 * i + s, s, h_s, guard=normed(k_h, n_in) if i + s == 0 else None,
                                 rides=first == S_FFN)
                with pe.Fori(done, n) as i:
                    slab(i * 2 + gu, 0, h_s)
                    slab(i * 2 + gu + 1, 1, h_s)

                def hidden(c):
                    pe.wait_ge(mid_ready, (first == S_FFN2) * (FB // 2) + pairs + -(-kt * (c + 1) // 2))
                slab(down, 0, mid_s, kt, guard=hidden)
                slab(down + 1, 1, mid_s, kt)
                with pe.Fori(1, OUT_SLABS // 2) as i:
                    slab(i * 2 + down, 0, mid_s, kt)
                    slab(i * 2 + down + 1, 1, mid_s, kt)
            if first == S_FFN2:
                sum_squares(n_sq)

        ffn(S_FFN, 1, 2, h_s, mid_s)

        def swap(j):
            pe.wait_ge(qkv_stored, j + 1)
            if j == 0:
                pe.wait_ge(tables_loaded, 16 * 5)
            if j >= 1:
                pe.wait_ge(rotated, j)
            pe.matmul(pm[0][0:ROT, :], perm[:, :], qk_m[0:ROT, 2 * (j % 4):2 * (j % 4) + 2, j // 4, :],
                      start=True, stop=True).then_inc(swapped, 1)

        def moba_scores(h):
            pe.wait_ge(rotated, 8)
            if h >= 1:
                pe.wait_ge(maxed, h)
            pe.matmul(pm[1][:, 0:P], qk_m[:, h, 0, 0:P], qk_m[:, h, 1, 0:P], start=True, stop=True)
            pe.matmul(pm[1][:, P:3 * P], qk_m[:, h, 0, P:T], qk_m[:, h, 1, :], start=True, stop=True)\
              .then_inc(scores_mm, 1)

        def moba_turn(h):
            pe.wait_ge(prob_ready, h + 1)
            if h >= 1:
                pe.wait_ge(prob_copied, h)
            pe.wait_ge(ident_loaded, 16)
            for j in range(3):
                mm = pe.transpose(pm[2][:, j * P:(j + 1) * P], prob[:, h % 2, j * P:(j + 1) * P], ident[:, :])
            mm.then_inc(turned, 1)

        def moba_out(h):
            pe.wait_ge(prob_copied, h + 1)
            pe.wait_ge(qkv_stored, 12)
            if h >= 1:
                pe.wait_ge(moba_ready, h)
            pe.matmul(pm[3][:, 0:T], v_m[:, 0, h * P:(h + 1) * P], prob_t[:, 0:T], start=True, stop=False)
            pe.matmul(pm[3][:, P:T], v_m[:, 1, h * P:(h + 1) * P], prob_t[:, T:3 * P], start=False, stop=True)\
              .then_inc(moba_mm, 1)

        def ret_score(h):
            pe.wait_ge(qkv_stored, 12 + 8)
            if h >= 1:
                pe.wait_ge(ret_decayed, h)
            for k in range(2):
                pe.matmul(pm[0][:, 0:T], qk_r[:, h, 1, k, 0:P], qk_r[:, h, 0, k, :], start=(k == 0), stop=(k == 1))
            for k in range(2):
                mm = pe.matmul(pm[0][:, T:3 * P], qk_r[:, h, 1, k, P:T], qk_r[:, h, 0, k, P:T],
                               start=(k == 0), stop=(k == 1))
            mm.then_inc(ret_scores, 1)

        def ret_out(h):
            pe.wait_ge(ret_decayed, h + 1)
            pe.wait_ge(qkv_stored, 12 + 8 + h + 1)
            if h >= 1:
                pe.wait_ge(ret_full, h)
            for e in range(2):
                c0 = h * RET_DIM + e * P
                pe.matmul(pm[1][:, e * T:(e + 1) * T], v_r[:, 0, c0:c0 + P], prob[:, h % 2, 0:T], start=True, stop=False)
                mm = pe.matmul(pm[1][:, e * T + P:(e + 1) * T], v_r[:, 1, c0:c0 + P], prob[:, h % 2, T:3 * P],
                               start=False, stop=True)
            mm.then_inc(ret_mm, 1)

        def ret_sum(h):
            pe.wait_ge(ret_squared, h + 1)
            if h >= 1:
                pe.wait_ge(ret_var, h)
            pe.matmul(pm[2][:, 0:T], ones[:, :], val[:, 0, 0, :], start=True, stop=False)
            pe.matmul(pm[2][:, 0:T], ones[:, :], val[:, 0, 1, :], start=False, stop=True).then_inc(ret_summed, 1)

        for q in range(IN2_SLABS):
            slab(S_IN2 + q, q % 2, h_s, guard=normed(2) if q == 0 else None, tok=q in V_SLABS,
                 after=lambda c: ret_out((q - 25) // 2) if 25 <= q <= 31 and q % 2 == 1 and c == 1 else None)
            if q == 0:
                sum_squares(2)
            if q == 2:
                pe.wait_ge(rstd_ready, 1)
                pe.wait_ge(ident_loaded, 16)
                for b in range(2):
                    mm = pe.matmul(pm[3][:, b:b + 1], rstd_h[:, b * P:(b + 1) * P], ident[:, 0:1], start=True, stop=True)
                mm.then_inc(rstd_turned, 1)
            if 1 <= q <= 8:
                swap(q - 1)
            if 0 <= q - 15 < 8:
                moba_out(q - 15)
            if 0 <= q - 14 < 8:
                moba_turn(q - 14)
            if 0 <= q - 12 < 8:
                moba_scores(q - 12)
            if 23 <= q <= 29 and q % 2 == 1:
                ret_score((q - 23) // 2)
            if 25 <= q <= 31 and q % 2 == 1:
                ret_sum((q - 25) // 2)

        pe.wait_ge(ret_ready, RET_HEADS)
        pe.wait_ge(moba_ready, MOBA_HEADS)
        with pe.Fori(0, OUT_SLABS) as m:
            for s, acts in ((0, o_r), (1, o_m)):
                pe.wait_ge(evacuated, m * 2 + S_MERGE + s - 1)
                for c in range(2):
                    multiply(m * CHUNKS + CHUNKS * S_MERGE + 2 * s + c, 2 * s + c, s, acts, c * KT, KT, c == 0, c == 1)
        offset[0] = OUT_SLABS

        def merged(c):
            pe.wait_ge(merged_ready, 2 * (c + 1))
        for q in range(2):
            slab(S_OUT2 + q, q, h_s, guard=merged if q == 0 else None)
        with pe.Fori(1, OUT_SLABS // 2) as i:
            slab(i * 2 + S_OUT2, 0, h_s)
            slab(i * 2 + S_OUT2 + 1, 1, h_s)
        ffn(S_FFN2, 3, 4, mid_s, h_s, n_in=3)

    @block.scalar
    def _(act):
        def convert(pair, s, c, kt=KT):
            G = 2 * CHUNKS * pair + CHUNKS * s + c
            act.wait_ge(raw_loaded[CHUNKS * s + c], 16 * (pair + 1))
            if not (isinstance(pair, int) and G < RING):
                act.wait_ge(chunk_used, G - RING + 1)
            act.activation(split[:, c, 0:kt, 0, :], raw[:, CHUNKS * s + c, 0:kt, :], ACT.Copy).then_inc(hi_ready, 1)

        def copy_low(E, s, used):
            act.wait_ge(chunk_used, used)
            if not (isinstance(E, int) and E < 2):
                act.wait_ge(evacuated, E - 1)
            act.activation(low[:, s, :, :], ps[:, s, :, T:2 * T], ACT.Copy).then_inc(low_copied, 1)

        offset = [0]

        def turn(pair, s, mid=None, kt_next=KT):
            for c in range(CHUNKS):
                if s == 0:
                    convert(pair, 1, c, kt_next)
                else:
                    convert(pair + 1, 0, c, kt_next)
                if mid is not None:
                    mid(c)
            S = 2 * pair + s
            copy_low(S + offset[0], s, CHUNKS * S + CHUNKS)

        def last_turn(pair, s):
            S = 2 * pair + s
            copy_low(S + offset[0], s, CHUNKS * S + CHUNKS)

        def turn_rows(S, c):
            for i, part in enumerate(RIDE_PARTS):
                if (TURN_AT[part], 1) == (S, c):
                    act.wait_ge(ada_turned, part + 1)
                    for j in range(2):
                        row = act.activation(acc[0:1, part % 2, j * 512:(j + 1) * 512], pm[j][0:1, :], ACT.Copy)
                    row.then_inc(row_copied, 1)
                    act.wait_ge(row_copied, i + 1)
                    act.dma_start(mod[:, part * 8:(part + 1) * 8], acc[0:1, part % 2, :]).then_inc(row_turned, 16)

        def square(n, j, pre=None):
            act.wait_ge(x_updated, OUT_SLABS * (n - 1) + j + 1)
            if pre is not None:
                k_h, dst, gains = pre
                for b in range(2 * j, 2 * j + 2):
                    act.activation(dst[:, b, 0, :], x_t[:, b, :], ACT.Copy, scale=gains[:, b:b + 1]).then_inc(norm_hi, 1)
                if k_h == 2:
                    for b in range(2):
                        sq = act.activation(sq_gf[:, j % 2, b, :], x_t[:, 2 * j + b, :], ACT.Square,
                                            scale=col("g_norm_final", 2 * j + b))
                    sq.then_inc(gf_squared, 1)
            act.activation(val[:, j % 2, :, :], x_t[:, 2 * j:2 * j + 2, :], ACT.Square).then_inc(squared, 1)

        def root(n):
            act.wait_ge(var_ready, n + 1)
            if n == 2:
                act.activation(rstd_h[:, :], rstd_h[:, :], ACT.Sqrt)
            act.activation(rstd[:, :], rstd[:, :], ACT.Sqrt).then_inc(std_ready, 1)

        def norm(n, k, shift, convert_first=False):
            if n > 0:
                root(n)
            for b in range(DB):
                act.wait_ge(norm_t, DB * k + b + 1)
                act.activation(h_s[:, b, 0, :], val4[:, b % 4, :], ACT.Identity,
                               bias=mod[:, shift * DB + b:shift * DB + b + 1]).then_inc(norm_hi, 1)
                if convert_first and b in (3, 7, 11):
                    convert(0, 0, (b + 1) // 4)

        act.wait_ge(params_loaded, 16)
        act.activation(c_act[:, :], col("c", 0, DB), ACT.Silu).then_inc(c_ready, 1)
        act.wait_ge(x_loaded, 16)
        for j in range(OUT_SLABS):
            if j >= 2:
                act.wait_ge(ssq_added, j - 1)
            act.activation(val[:, j % 2, :, :], x_t[:, 2 * j:2 * j + 2, :], ACT.Square).then_inc(squared, 1)
        root(0)
        act.wait_ge(lam_abs, 1)
        act.activation(lam_e[:, :], lam_p[:, :], ACT.Exp, scale=-1.0).then_inc(lam_exp, 1)
        convert(0, 0, 0)
        norm(0, 0, 0, convert_first=True)

        def sigmoids(q):
            act.wait_ge(gates_mm, q + 1)
            for b in range(2):
                blk = 2 * q + b
                act.activation(gate_r[:, blk, :], pm[b][:, 0:T], ACT.Sigmoid, bias=col("b_rg_a", blk))
                last = act.activation(gate_i[:, blk, :], pm[b][:, T:2 * T], ACT.Sigmoid, bias=col("b_rg_i", blk))
            last.then_inc(gates_read, 1)

        def lru_decay(half):
            if half == 0:
                act.wait_ge(lam_ready, 1)
                act.wait_ge(gates_read, 4)
                act.wait_ge(conv_ready, 4)
            for blk in range(4 * half, 4 * half + 4):
                act.activation(lru_t[:, blk, :], gate_r[:, blk, :], ACT.Tanh, scale=lam_n8[:, blk:blk + 1])
            for blk in range(4 * half, 4 * half + 4):
                last = act.activation(gate_r[:, blk, :], gate_r[:, blk, :], ACT.Exp, scale=lam_8[:, blk:blk + 1])
            last.then_inc(decays, 1)

        def first_mid(q):
            def mid(c):
                turn_rows(S_IN + q, c)
                if c == 0 and 2 <= q <= 5:
                    sigmoids(q - 2)
                if c == 2 and q in (5, 6):
                    lru_decay(q - 5)
                if c == 0 and q in (7, 8):
                    half = q - 7
                    act.wait_ge(mult_sq, half + 1)
                    act.activation(lru_t[:, 4 * half:4 * half + 4, :], lru_t[:, 4 * half:4 * half + 4, :], ACT.Sqrt)\
                       .then_inc(mult_ready, 1)
                if c == 1 and 6 <= q <= 9:
                    pool_high(q - 6)
                if c == 0 and q >= 9:
                    gelu(q - 9)
                if c == 2 and q >= 9:
                    y_high(q - 9)
            return mid

        def gelu(j):
            act.wait_ge(evacuated, 8 + j + 1)
            act.activation(val[:, j % 2, :, :], val[:, j % 2, :, :], ACT.Gelu_apprx_tanh).then_inc(gelu_ready, 1)

        def y_high(j):
            act.wait_ge(y_full, j + 1)
            act.activation(mid_s[:, LB + 2 * j:LB + 2 * j + 2, 0, :], xc[:, 2 * j:2 * j + 2, :], ACT.Copy).then_inc(y_hi, 1)

        def pool_high(g):
            act.wait_ge(pool_mm, g + 1)
            if g == 1:
                act.wait_ge(mult_sq, 2)
            for b in range(2):
                ins = act.activation(mid_s[:, 2 * g + b, 0, :], pm[2][:, b * T:(b + 1) * T], ACT.Copy,
                                     scale=col("ls_pool", 2 * g + b))
            ins.then_inc(pool_hi, 1)

        for q in range(IN_SLABS):
            turn(q // 2, q % 2, mid=first_mid(q))
        gelu(3)
        y_high(3)
        for q in range(OUT_SLABS):
            def mid(c):
                if c == 0 and q >= 1:
                    square(1, q - 1)
                turn_rows(S_OUT + q, c)
            turn((S_OUT + q) // 2, q % 2, mid)
        square(1, OUT_SLABS - 1)
        norm(1, 1, 3)

        def ffn(first, n_sq, pre=None):
            for g, gu, n, down, kt, pairs in groups(first):
                def hidden_pair(i, kt_next=KT, mid=None):
                    pair = i + gu // 2

                    def up_mid(c):
                        if c == 0 and first == S_FFN:
                            act.wait_ge(evacuated, pair * 2 + 1)
                            act.activation(val[:, 0, :, :], val[:, 0, :, :], ACT.Silu).then_inc(act_done, 1)
                        elif c == 0:
                            act.wait_ge(val_ready, i + (pairs + 1))
                            act.activation(conv_o[:, 0, :, :], conv_o[:, 0, :, :], ACT.Silu).then_inc(act_done, 1)
                        if mid is not None:
                            mid(2 * i + 1, c)
                    turn(pair, 0, mid=mid and (lambda c: mid(2 * i, c)))
                    turn(pair, 1, mid=up_mid, kt_next=kt_next)
                done = 0
                if first == S_FFN and g == 0:
                    done = (RIDE_SLABS + 2 - S_FFN) // 2
                    for i in range(done):
                        hidden_pair(i, mid=lambda slab, c: turn_rows(S_FFN + slab, c))
                elif g == 0:
                    done = 1
                    hidden_pair(0, mid=lambda slab, c: root(3) if (slab, c) == (0, 2) else None)
                with act.Fori(done, n - 1) as i:
                    hidden_pair(i)
                hidden_pair(n - 1, kt)
                last_group = g == len(FFN_GROUPS) - 1
                if not last_group:
                    with act.Fori(0, OUT_SLABS // 2) as i:
                        turn(i + down // 2, 0)
                        turn(i + down // 2, 1)
                else:
                    for q in range(OUT_SLABS):
                        def mid(c):
                            if c == 0 and q >= 1:
                                square(n_sq, q - 1, pre)
                        if q < OUT_SLABS - 1:
                            turn((down + q) // 2, q % 2, mid, kt_next=kt)
                        elif down + q + 1 < S_END:
                            turn((down + q) // 2, q % 2, mid)
                        else:
                            square(n_sq, q - 1)
                            last_turn((down + q) // 2, q % 2)
                    square(n_sq, OUT_SLABS - 1, pre)

        ffn(S_FFN, 2, (2, h_s, gain))

        def moba_exp(h):
            act.wait_ge(maxed, h + 1)
            act.activation(prob[:, h % 2, 0:P], prob[:, h % 2, 0:P], ACT.Exp, bias=s_neg[:, 0:1], scale=MOBA_DIM ** -0.5,
                           accum_out=s_sum[:, 0:1])
            act.activation(prob[:, h % 2, P:3 * P], prob[:, h % 2, P:3 * P], ACT.Exp, bias=s_neg[:, 1:2], scale=MOBA_DIM ** -0.5,
                           accum_out=s_sum[:, 1:2]).then_inc(exped, 1)

        def moba_copy(h):
            act.wait_ge(turned, h + 1)
            if h >= 1:
                act.wait_ge(moba_mm, h)
            act.activation(prob_t[:, :], pm[2][:, 0:3 * P], ACT.Copy).then_inc(prob_copied, 1)

        def moba_high(h):
            act.wait_ge(moba_mm, h + 1)
            act.activation(o_m[:, h, 0, :], pm[3][:, 0:T], ACT.Copy).then_inc(moba_hi, 1)

        def ret_square(h):
            act.wait_ge(ret_mm, h + 1)
            act.wait_ge(act_done, FB // 2 + min(2 * h + 1, 4) + max(2 * h - 3, 0))
            act.activation(val[:, 0, :, :].rearrange("p b t -> p (b t)"), pm[1][:, :], ACT.Square).then_inc(ret_squared, 1)

        def ret_root(h):
            act.wait_ge(ret_var, h + 1)
            act.activation(rstd[:, :], rstd[:, :], ACT.Sqrt).then_inc(ret_std, 1)

        def ret_high(h):
            act.wait_ge(ret_full, h + 1)
            act.activation(o_r[:, 2 * h:2 * h + 2, 0, :], val[:, 0, :, :], ACT.Copy).then_inc(ret_hi, 1)

        def second_mid(q):
            def mid(c):
                if q == 0 and c == 3:
                    root(2)
                if c == 1 and 0 <= q - 13 < 8:
                    moba_exp(q - 13)
                if c == 0 and 0 <= q - 15 < 8:
                    moba_copy(q - 15)
                if c == 0 and 0 <= q - 16 < 8:
                    moba_high(q - 16)
                if 25 <= q <= 31 and q % 2 == 1 and c == 2:
                    ret_square((q - 25) // 2)
                if 26 <= q <= 32 and q % 2 == 0 and c == 0:
                    ret_root((q - 26) // 2)
                if 26 <= q <= 32 and q % 2 == 0 and c == 3:
                    ret_high((q - 26) // 2)
            return mid

        for q in range(IN2_SLABS):
            turn((S_IN2 + q) // 2, q % 2, mid=second_mid(q))
            if 24 <= q < 28:
                act.wait_ge(qkv_stored, q + 1)
                act.activation(g_r[:, 2 * (q - 24):2 * (q - 24) + 2, :], g_r[:, 2 * (q - 24):2 * (q - 24) + 2, :],
                               ACT.Silu).then_inc(act_done, 1)
            if q >= 28:
                k = q - 28
                sg, j = (sig_r, k) if k < 8 else (sig_m, k - 8)
                act.wait_ge(evacuated, S_IN2 + q + 1)
                act.activation(sg[:, 2 * j:2 * j + 2, :], val[:, q % 2, :, :], ACT.Sigmoid).then_inc(act_done, 1)

        for m in range(OUT_SLABS):
            pair, s = (S_MERGE + m) // 2, m % 2
            for c in range(CHUNKS):
                if s == 0:
                    convert(pair, 1, c)
                else:
                    convert(pair + 1, 0, c)
                if c == 1:
                    copy_low(S_MERGE + 2 * m, 0, CHUNKS * (S_MERGE + m) + 2)
            copy_low(S_MERGE + 2 * m + 1, 1, CHUNKS * (S_MERGE + m) + 4)
            act.wait_ge(merged_t, m + 1)
            act.activation(h_s[:, 2 * m:2 * m + 2, 0, :], val[:, 0, :, :], ACT.Copy).then_inc(merged_hi, 1)
        offset[0] = OUT_SLABS
        pre_2 = (3, mid_s, col("ffn_norm_w_2", 0, DB))
        for q in range(OUT_SLABS):
            turn((S_OUT2 + q) // 2, q % 2, lambda c: square(3, q - 1, pre_2) if c == 0 and q >= 1 else None)
        square(3, OUT_SLABS - 1, pre_2)
        ffn(S_FFN2, 4)
        root(4)

    @block.vector
    def _(dve):
        steps = Steps()

        def own(ins):
            ins.then_inc(dve_step, 1)
            dve.wait_ge(dve_step, steps.next())

        def convert(pair, s, c, kt=KT):
            G = 2 * CHUNKS * pair + CHUNKS * s + c
            dve.wait_ge(hi_ready, G + 1)
            dve.tensor_tensor(split[:, c, 0:kt, 1, :], raw[:, CHUNKS * s + c, 0:kt, :],
                              split[:, c, 0:kt, 0, :].bitcast(F32), ALU.subtract).then_inc(lo_ready, 1)

        def evacuate(E, s, dst, scale=None):
            dve.wait_ge(low_copied, E + 1)
            both = low[:, s, :, :]
            if scale is None:
                ins = dve.tensor_tensor(dst, ps[:, s, :, 0:T], both, ALU.add)
            else:
                own(dve.tensor_tensor(both, ps[:, s, :, 0:T], both, ALU.add))
                if scale == "columns":
                    for b in range(2):
                        ins = dve.tensor_scalar(dst[:, b, :], both[:, b, :], rstd_col[:, b:b + 1], None, ALU.mult)
                else:
                    ins = dve.tensor_tensor(dst, both, scale[:, :].unsqueeze(1).to_broadcast([P, 2, T]), ALU.mult)
            ins.then_inc(evacuated, 1)
            dve.wait_ge(evacuated, E + 1)

        offset = [0]

        def turn(pair, s, dst, mid=None, kt_next=KT, scale=None):
            for c in range(CHUNKS):
                if s == 0:
                    convert(pair, 1, c, kt_next)
                else:
                    convert(pair + 1, 0, c, kt_next)
                if mid is not None:
                    mid(c)
            evacuate(2 * pair + s + offset[0], s, dst, scale)

        def add_ada(part, k, first, piece, loaded, times, added):
            sums = acc[:, part % 2, :]
            dve.wait_ge(loaded, 16 * times)
            if first:
                if part >= ADA_FIRST + 2:
                    dve.wait_ge(row_turned, 16 * (part - 1 - ADA_FIRST))
                elif part >= 2:
                    dve.wait_ge(ada_turned, part - 1)
                dve.tensor_scalar(sums, piece, c_act[:, k:k + 1], None, ALU.mult).then_inc(ada_added, 1)
            else:
                dve.wait_ge(ada_added, added - 1)
                dve.scalar_tensor_tensor(out=sums, in0=piece, scalar=c_act[:, k:k + 1], in1=sums,
                                         op0=ALU.mult, op1=ALU.add).then_inc(ada_added, 1)

        def add_first(part, k):
            slot = k % ADA_RING
            add_ada(part, k, k == 0, ada[:, slot, :], ada_loaded[slot], part * (DB // ADA_RING) + (k // ADA_RING + 1),
                    part * DB + k + 1)

        def finish_rows(S):
            for i, part in enumerate(RIDE_PARTS):
                if TURN_AT[part] + 1 == S:
                    dve.wait_ge(row_turned, 16 * (i + 1))
                    dve.tensor_tensor(mod[:, part * 8:part * 8 + 8], mod[:, part * 8:part * 8 + 8],
                                      col("b_ada", part * 8, 8), ALU.add).then_inc(mod_ready, 1)

        def add_rides(S, c):
            if c == 0 and S != S_FFN:
                finish_rows(S)
            for piece, at in enumerate(RIDE_AT):
                if at == (S, c, "vector"):
                    part, slot = ADA_FIRST + piece // DB, piece % RIDE_RING
                    add_ada(part, piece % DB, piece == _pieces(part, "vector")[0], ride[:, slot, :], ride_loaded[slot],
                            piece // RIDE_RING + 1, PIECE_COUNT[piece])

        def finish_ada(part, parity):
            dve.wait_ge(ada_turned, part + 1)
            a = PARAMS["b_ada"][0]
            dve.tensor_tensor(mod[:, part * 8:part * 8 + 8], pm[3][:, 8 * parity:8 * parity + 8],
                              par[:, part * 8 + a:part * 8 + a + 8], ALU.add).then_inc(mod_ready, 1)

        def add_squares(n, j):
            dve.wait_ge(squared, OUT_SLABS * n + j + 1)
            if j == 0:
                dve.tensor_copy(ssq[:, :, :], val[:, 0, :, :]).then_inc(ssq_added, 1)
            else:
                dve.wait_ge(ssq_added, OUT_SLABS * n + j)
                dve.tensor_tensor(ssq[:, :, :], ssq[:, :, :], val[:, j % 2, :, :], ALU.add).then_inc(ssq_added, 1)

        def variance(n):
            dve.wait_ge(ssq_summed, n + 1)
            var = dve.tensor_scalar(rstd[:, :], pm[2][:, 0:T], 1.0 / D, EPS, ALU.mult, ALU.add)
            if n == 2:
                own(dve.tensor_scalar(rstd_h[:, :], pm[2][:, T:2 * T], 1.0 / D, None, ALU.mult))
                var = dve.scalar_tensor_tensor(out=rstd_h[:, :], in0=rstd[:, :], scalar=EPS, in1=rstd_h[:, :],
                                               op0=ALU.mult, op1=ALU.add)
            var.then_inc(var_ready, 1)

        def inverse(n):
            dve.wait_ge(std_ready, n + 1)
            own(dve.reciprocal(rstd[:, :], rstd[:, :]))

        def inv_rms(n):
            variance(n)
            inverse(n)

        def norm(n, k, shift, convert_first=False):
            if n > 0:
                inv_rms(n)

            def lo(b):
                dve.wait_ge(norm_hi, DB * k + b + 1)
                dve.scalar_tensor_tensor(out=h_s[:, b, 1, :], in0=val4[:, b % 4, :],
                                         scalar=mod[:, shift * DB + b:shift * DB + b + 1],
                                         in1=h_s[:, b, 0, :].bitcast(F32), op0=ALU.add, op1=ALU.subtract).then_inc(h_ready, 1)
            for b in range(DB):
                if b >= 4:
                    dve.wait_ge(h_ready, DB * k + b - 3)
                dve.scalar_tensor_tensor(out=val4[:, b % 4, :], in0=x_t[:, b, :], scalar=gain[:, b:b + 1],
                                         in1=rstd[:, :], op0=ALU.mult, op1=ALU.mult).then_inc(norm_t, 1)
                if b >= 1:
                    lo(b - 1)
                if convert_first and b in (4, 8, 12):
                    convert(0, 0, b // 4)
            lo(DB - 1)
            dve.wait_ge(h_ready, DB * (k + 1))

        def residual(S, gate, k, dst_val):
            for b in range(2):
                xs = x_t[:, 2 * k + b, :]
                if gate is None:
                    ins = dve.tensor_tensor(xs, xs, dst_val[:, b, :], ALU.add)
                else:
                    ins = dve.scalar_tensor_tensor(out=xs, in0=dst_val[:, b, :],
                                                   scalar=mod[:, gate * DB + 2 * k + b:gate * DB + 2 * k + b + 1],
                                                   in1=xs, op0=ALU.mult, op1=ALU.add)
            return ins

        dve.wait_ge(params_loaded, 16)
        dve.wait_ge(c_ready, 1)
        dve.wait_ge(x_loaded, 16)
        for j in range(OUT_SLABS):
            add_squares(0, j)
        for k in range(DB):
            add_first(0, k)
        inv_rms(0)
        for k in range(DB):
            add_first(1, k)
            if k == 4:
                finish_ada(0, 0)
        lam = col("lru_lambda", 0, LB)
        dve.scalar_tensor_tensor(out=lam_p[:, :], in0=lam, scalar=-1.0, in1=lam, op0=ALU.mult, op1=ALU.max)\
           .then_inc(lam_abs, 1)
        dve.wait_ge(lam_exp, 1)
        own(dve.tensor_scalar(lam_z[:, :], lam_e[:, :], 2.0, None, ALU.add))
        own(dve.reciprocal(lam_z[:, :], lam_z[:, :]))
        own(dve.tensor_tensor(lam_z[:, :], lam_z[:, :], lam_e[:, :], ALU.mult))
        own(dve.tensor_tensor(lam_q[:, :], lam_z[:, :], lam_z[:, :], ALU.mult))
        own(dve.tensor_scalar(lam_p[:, :], lam_q[:, :], 1.0 / 17, None, ALU.mult))
        for n in (15, 13, 11, 9, 7, 5, 3):
            own(dve.scalar_tensor_tensor(out=lam_p[:, :], in0=lam_p[:, :], scalar=1.0 / n, in1=lam_q[:, :],
                                         op0=ALU.add, op1=ALU.mult))
        own(dve.scalar_tensor_tensor(out=lam_p[:, :], in0=lam_p[:, :], scalar=1.0, in1=lam_z[:, :],
                                     op0=ALU.add, op1=ALU.mult))
        own(dve.tensor_scalar(lam_e[:, :], lam, 0.0, None, ALU.min))
        own(dve.scalar_tensor_tensor(out=lam_z[:, :], in0=lam_p[:, :], scalar=-2.0, in1=lam_e[:, :],
                                     op0=ALU.mult, op1=ALU.add))
        own(dve.tensor_scalar(lam_8[:, :], lam_z[:, :], LRU_C, None, ALU.mult))
        dve.tensor_scalar(lam_n8[:, :], lam_z[:, :], -LRU_C, None, ALU.mult).then_inc(lam_ready, 1)

        for part in range(2, ADA_FIRST):
            for k in range(DB):
                add_first(part, k)
                if k == 4:
                    finish_ada(part - 1, 1 - part % 2)
        convert(0, 0, 0)
        finish_ada(ADA_FIRST - 1, 1)
        dve.wait_ge(mod_ready, 4)

        def modulated_gain(scale, name):
            own(dve.scalar_tensor_tensor(out=gain[:, :], in0=mod[:, scale * DB:(scale + 1) * DB], scalar=1.0,
                                         in1=col(name, 0, DB), op0=ALU.add, op1=ALU.mult))

        modulated_gain(1, "g_norm_mix")
        norm(0, 0, 0, convert_first=True)

        def conv(q):
            for j in range(CONV):
                tap = CONV - 1 - j
                for b in range(2):
                    blk = 2 * q + b
                    src = xr_pad[:, blk, tap:tap + T]
                    w = col("w_conv", tap * LB + blk)
                    if j == 0:
                        ins = dve.tensor_scalar(xc[:, blk, :], src, w, col("b_conv", blk), ALU.mult, ALU.add)
                    else:
                        ins = dve.scalar_tensor_tensor(out=xc[:, blk, :], in0=src, scalar=w, in1=xc[:, blk, :],
                                                       op0=ALU.mult, op1=ALU.add)
                if j < CONV - 1:
                    own(ins)
            ins.then_inc(conv_ready, 1)

        def multiplier(half):
            r = slice(4 * half, 4 * half + 4)
            buf = a_sq[:, :, :]
            dve.wait_ge(decays, half + 1)
            own(dve.tensor_tensor(buf, gate_r[:, r, :], gate_r[:, r, :], ALU.mult))
            dve.scalar_tensor_tensor(out=lru_t[:, r, :].rearrange("p b t -> p (b t)"), in0=buf.rearrange("p b t -> p (b t)"),
                                     scalar=1.0, in1=lru_t[:, r, :].rearrange("p b t -> p (b t)"),
                                     op0=ALU.add, op1=ALU.mult).then_inc(mult_sq, 1)

        def input_gate(half):
            r = slice(4 * half, 4 * half + 4)
            own(dve.tensor_tensor(gate_i[:, r, :], gate_i[:, r, :], xc[:, r, :], ALU.mult))

        def recurrence(half):
            r = slice(4 * half, 4 * half + 4)
            dve.wait_ge(mult_ready, half + 1)
            own(dve.tensor_tensor(gate_i[:, r, :], gate_i[:, r, :], lru_t[:, r, :], ALU.mult))
            for blk in range(4 * half, 4 * half + 4):
                ins = dve.tensor_tensor_scan(out=xc[:, blk, :], data0=gate_r[:, blk, :], data1=gate_i[:, blk, :],
                                             initial=0.0, op0=ALU.mult, op1=ALU.add)
            own(ins)

        def gated(j):
            dve.wait_ge(gelu_ready, j + 1)
            dve.tensor_tensor(xc[:, 2 * j:2 * j + 2, :], xc[:, 2 * j:2 * j + 2, :], val[:, j % 2, :, :], ALU.mult)\
               .then_inc(y_full, 1)

        def y_low(j):
            dve.wait_ge(y_hi, j + 1)
            dve.tensor_tensor(mid_s[:, LB + 2 * j:LB + 2 * j + 2, 1, :], xc[:, 2 * j:2 * j + 2, :],
                              mid_s[:, LB + 2 * j:LB + 2 * j + 2, 0, :].bitcast(F32), ALU.subtract).then_inc(y_ready, 1)

        def windows(g):
            w = WINDOWS[g]
            bufs = (pool_a, pool_b)
            src, n = pool_x, 1
            for j in range(g + 1):
                dst = bufs[j % 2]
                own(dve.tensor_tensor(dst[:, :, WPAD:], src[:, :, WPAD:], src[:, :, WPAD - n:WPAD - n + T], ALU.add))
                src, n = dst, 2 * n
            head = src[:, :, WPAD:WPAD + w - 1]
            for b in range(2):
                ins = dve.tensor_tensor(val[:, g % 2, b, 0:w - 1], head[:, b, :], inv_n[:, 0:w - 1], ALU.mult)
            own(ins)
            own(dve.tensor_tensor(val[:, g % 2, :, 0:w - 1], val[:, g % 2, :, 0:w - 1],
                                  pool_x[:, :, WPAD:WPAD + w - 1], ALU.subtract))
            dve.scalar_tensor_tensor(out=val[:, g % 2, :, w - 1:T], in0=src[:, :, WPAD + w - 1:WPAD + T], scalar=1.0 / w,
                                     in1=pool_x[:, :, WPAD + w - 1:WPAD + T], op0=ALU.mult, op1=ALU.subtract)\
               .then_inc(pooled, 1)
            dve.wait_ge(pooled, g + 1)

        def pool_low(g):
            dve.wait_ge(pool_hi, g + 1)
            for b in range(2):
                ins = dve.scalar_tensor_tensor(out=mid_s[:, 2 * g + b, 1, :], in0=pm[2][:, b * T:(b + 1) * T],
                                               scalar=col("ls_pool", 2 * g + b), in1=mid_s[:, 2 * g + b, 0, :].bitcast(F32),
                                               op0=ALU.mult, op1=ALU.subtract)
            ins.then_inc(pool_ready, 1)

        def first_mid(q):
            def mid(c):
                add_rides(S_IN + q, c)
                if c == 0 and q in (6, 7):
                    multiplier(q - 6)
                if c == 2 and q in (6, 7):
                    input_gate(q - 6)
                if c == 1 and q in (8, 9):
                    recurrence(q - 8)
                if c == 1 and 6 <= q <= 9:
                    pool_low(q - 6)
                if c == 1 and q >= 9:
                    gated(q - 9)
                if c == 3 and q >= 9:
                    y_low(q - 9)
            return mid

        dve.wait_ge(constants, 22)
        own(dve.memset(pool_b[:, :, 0:WPAD], 0.0))
        for q in range(IN_SLABS):
            if q < 4:
                dst = xr_pad[:, 2 * q:2 * q + 2, PAD:]
            elif q < 8:
                dst = pool_x[:, :, WPAD:]
            else:
                dst = val[:, q % 2, :, :]
            turn(q // 2, q % 2, dst, mid=first_mid(q))
            if q < 4:
                conv(q)
            elif q < 8:
                windows(q - 4)
        gated(3)

        def pre_low(pre, j):
            k_h, dst, gains = pre
            for b in range(2 * j, 2 * j + 2):
                dve.wait_ge(norm_hi, DB * k_h + b + 1)
                dve.scalar_tensor_tensor(out=dst[:, b, 1, :], in0=x_t[:, b, :], scalar=gains[:, b:b + 1],
                                         in1=dst[:, b, 0, :].bitcast(F32), op0=ALU.mult, op1=ALU.subtract).then_inc(h_ready, 1)

        def gained(j):
            for b in range(2 * j, 2 * j + 2):
                dve.tensor_scalar(out_t[:, b, :], x_t[:, b, :], col("final_norm_w_2", b), None, ALU.mult)

        def add_gf_squares(j):
            dve.wait_ge(gf_squared, j + 1)
            if j == 0:
                dve.tensor_copy(ssq_gf[:, :, :], sq_gf[:, 0, :, :]).then_inc(gf_added, 1)
            else:
                dve.wait_ge(gf_added, j)
                dve.tensor_tensor(ssq_gf[:, :, :], ssq_gf[:, :, :], sq_gf[:, j % 2, :, :], ALU.add).then_inc(gf_added, 1)

        def residual_turn(S, k, gate, n_norm, pair, s, kt_next=KT, mid=None, last=False, pre=None):
            two = pre is not None and pre[0] == 2
            end = n_norm == 4
            late = two and k == OUT_SLABS - 1

            def both(c):
                if c == 1 and k >= 1:
                    if pre is not None:
                        pre_low(pre, k - 1)
                    if not late:
                        add_squares(n_norm, k - 1)
                    if end:
                        gained(k - 1)
                if c == 2 and k >= 1 and two and not late:
                    add_gf_squares(k - 1)
                if mid is not None:
                    mid(c)
            if last:
                both(1)
                evacuate(2 * pair + s + offset[0], s, val[:, s, :, :])
            else:
                turn(pair, s, val[:, s, :, :], mid=both, kt_next=kt_next)
            residual(S, gate, k, val[:, s]).then_inc(x_updated, 1)
            if k == OUT_SLABS - 1:
                if pre is not None:
                    pre_low(pre, k)
                if late:
                    add_squares(n_norm, k - 1)
                    add_gf_squares(k - 1)
                    add_gf_squares(k)
                add_squares(n_norm, k)
                if end:
                    gained(k)

        def out_mid(q):
            def mid(c):
                if c == 0 and q == 0:
                    y_low(3)
                add_rides(S_OUT + q, c)
            return mid
        dve.wait_ge(mod_ready, 6)
        for q in range(OUT_SLABS):
            residual_turn(S_OUT + q, q, 2, 1, (S_OUT + q) // 2, q % 2, mid=out_mid(q))
        finish_rows(S_FFN)
        dve.wait_ge(mod_ready, 10)
        modulated_gain(4, "g_norm_ffn")
        norm(1, 1, 3)

        def conv_2(s, i):
            base = s * FB
            for j in range(CONV_2):
                tap = CONV_2 - 1 - j
                for b in range(2):
                    src = up_pad[:, s, b, tap:tap + T]
                    k = i * 2 + (base + b)
                    w = par[:, bass.ds(k + (PARAMS["conv_w_2"][0] + tap * 2 * FB), 1)]
                    dst = conv_o[:, s, b, :]
                    if j == 0:
                        bias = par[:, bass.ds(k + PARAMS["conv_b_2"][0], 1)]
                        ins = dve.tensor_scalar(dst, src, w, bias, ALU.mult, ALU.add)
                    else:
                        ins = dve.scalar_tensor_tensor(out=dst, in0=src, scalar=w, in1=dst, op0=ALU.mult, op1=ALU.add)
                if j < CONV_2 - 1:
                    own(ins)
            return ins

        def ffn(first, n_sq, gate, mid_s=mid_s, pre=None):
            scale = rstd if first == S_FFN2 else None
            for g, gu, n, down, kt, pairs in groups(first):
                h0 = (first == S_FFN2) * (FB // 2) + pairs

                def hidden_pair(i, kt_next=KT, mid=None):
                    pair = i + gu // 2
                    h = i + h0
                    if first == S_FFN:
                        turn(pair, 0, val[:, 0, :, :], mid=mid and (lambda c: mid(2 * i, c)))
                        turn(pair, 1, val[:, 1, :, :], mid=mid and (lambda c: mid(2 * i + 1, c)), kt_next=kt_next)
                        a, b = val[:, 0, :, :], val[:, 1, :, :]
                    else:
                        turn(pair, 0, up_pad[:, 0, :, PAD_2:], mid=mid, scale=scale)
                        conv_2(0, i + pairs).then_inc(val_ready, 1)
                        turn(pair, 1, up_pad[:, 1, :, PAD_2:], kt_next=kt_next, scale=scale)
                        own(conv_2(1, i + pairs))
                        a, b = conv_o[:, 0, :, :], conv_o[:, 1, :, :]
                    dve.wait_ge(act_done, h + 1 + act_before)
                    hid = (lambda part: mid_s[:, 2 * i:2 * i + 2, part, :]) if isinstance(i, int) else \
                        (lambda part: mid_s[:, bass.ds(i * 2, 2), part, :])
                    dve.tensor_tensor(hid(0), a, b, ALU.mult)
                    own(dve.tensor_tensor(b, a, b, ALU.mult))
                    dve.tensor_tensor(hid(1), b, hid(0).bitcast(F32), ALU.subtract).then_inc(mid_ready, 1)

                act_before = 0 if first == S_FFN else 4 + 16
                done = 0
                if first == S_FFN and g == 0:
                    done = (RIDE_SLABS + 2 - S_FFN) // 2
                    for i in range(done):
                        def mid(slab, c):
                            add_rides(S_FFN + slab, c)
                        hidden_pair(i, mid=mid)
                elif g == 0:
                    def mid(c):
                        if c == 2:
                            variance(3)
                        if c == 3:
                            inverse(3)
                    done = 1
                    hidden_pair(0, mid=mid)
                per = 1 if first == S_FFN else 2 * (CONV_2 - 1) + 4
                with dve.Fori(done, n - 1) as i:
                    steps.enter(i - done, per)
                    hidden_pair(i)
                steps.leave(n - 1 - done)
                hidden_pair(n - 1, kt)
                if g == 0 and gate is not None:
                    dve.wait_ge(mod_ready, ADA_PARTS)
                if g < len(FFN_GROUPS) - 1:
                    with dve.Fori(0, OUT_SLABS // 2) as i:
                        for s in range(2):
                            turn(i + down // 2, s, val[:, s, :, :])
                            for b in range(2):
                                k = i * 4 + (2 * s + b)
                                xs = x_t[:, bass.ds(k, 1), :].rearrange("p b t -> p (b t)")
                                if gate is None:
                                    dve.tensor_tensor(xs, xs, val[:, s, b, :], ALU.add)
                                else:
                                    dve.scalar_tensor_tensor(out=xs, in0=val[:, s, b, :],
                                                             scalar=mod[:, bass.ds(k + gate * DB, 1)],
                                                             in1=xs, op0=ALU.mult, op1=ALU.add)
                else:
                    for q in range(OUT_SLABS):
                        end = down + q + 1 == S_END
                        residual_turn(down + q, q, gate, n_sq, (down + q) // 2, q % 2,
                                      kt_next=kt if q < OUT_SLABS - 1 else KT, last=end, pre=pre)

        own(dve.tensor_tensor(gain[:, :], col("g_norm_final", 0, DB), col("attn_norm_w_2", 0, DB), ALU.mult))
        ffn(S_FFN, 2, 5, pre=(2, h_s, gain))

        def final_x(k):
            for b in range(2 * k, 2 * k + 2):
                dve.scalar_tensor_tensor(out=x_t[:, b, :], in0=x_t[:, b, :], scalar=col("g_norm_final", b),
                                         in1=rstd[:, :], op0=ALU.mult, op1=ALU.mult)
        def rotate_m(j):
            dve.wait_ge(swapped, j + 1)
            xs = qk_m[0:ROT, 2 * (j % 4):2 * (j % 4) + 2, j // 4, :]
            cos = rope_m[:, 0:1, :].to_broadcast([ROT, 2, T])
            sin = rope_m[:, 1:2, :].to_broadcast([ROT, 2, T])
            t = val[0:ROT, 0, :, :]
            own(dve.tensor_tensor(t, pm[0][0:ROT, :].rearrange("p (b t) -> p b t", b=2), sin, ALU.mult))
            own(dve.tensor_tensor(xs, xs, cos, ALU.mult))
            dve.tensor_tensor(xs, xs, t, ALU.add).then_inc(rotated, 1)

        def rotate_r(h, which):
            xs = qk_r[:, h, which, :, :]
            cos = rope_r[:, 0:1, :].to_broadcast([P, 2, T])
            sin = rope_r[:, 1:2, :].to_broadcast([P, 2, T])
            dve.tensor_tensor(val[:, 0, :, :], xs, cos, ALU.mult)
            own(dve.tensor_tensor(val[:, 1, :, :], xs, sin, ALU.mult))
            dve.tensor_tensor(xs[:, 0, :], val[:, 0, 0, :], val[:, 1, 1, :], ALU.subtract)
            return dve.tensor_tensor(xs[:, 1, :], val[:, 0, 1, :], val[:, 1, 0, :], ALU.add)

        def moba_max(h):
            dve.wait_ge(scores_mm, h + 1)
            if h >= 2:
                dve.wait_ge(turned, h - 1)
            own(dve.tensor_tensor(prob[:, h % 2, :], pm[1][:, 0:3 * P], cmask[:, :], ALU.min))
            dve.tensor_reduce(s_max[:, 0:1], prob[:, h % 2, 0:P], AX.X, ALU.max)
            own(dve.tensor_reduce(s_max[:, 1:2], prob[:, h % 2, P:3 * P], AX.X, ALU.max))
            dve.tensor_scalar(s_neg[:, :], s_max[:, :], -(MOBA_DIM ** -0.5), None, ALU.mult).then_inc(maxed, 1)

        def moba_softmax(h):
            dve.wait_ge(exped, h + 1)
            own(dve.reciprocal(s_inv[:, :], s_sum[:, :]))
            dve.tensor_scalar(prob[:, h % 2, 0:P], prob[:, h % 2, 0:P], s_inv[:, 0:1], None, ALU.mult)
            dve.tensor_scalar(prob[:, h % 2, P:3 * P], prob[:, h % 2, P:3 * P], s_inv[:, 1:2], None, ALU.mult).then_inc(prob_ready, 1)

        def moba_low(h):
            dve.wait_ge(moba_hi, h + 1)
            dve.tensor_tensor(o_m[:, h, 1, :], pm[3][:, 0:T], o_m[:, h, 0, :].bitcast(F32), ALU.subtract)\
               .then_inc(moba_ready, 1)

        def ret_decay(h):
            dve.wait_ge(ret_scores, h + 1)
            if h == 0:
                dve.wait_ge(turned, MOBA_HEADS)
            else:
                dve.wait_ge(ret_mm, h)
            dve.tensor_tensor(prob[:, h % 2, 0:T], pm[0][:, 0:T], decay[:, h, :], ALU.mult)
            dve.tensor_tensor(prob[:, h % 2, T:3 * P], pm[0][:, T:3 * P], decay[:, h, 0:P], ALU.mult).then_inc(ret_decayed, 1)

        def ret_variance(h):
            dve.wait_ge(ret_summed, h + 1)
            dve.tensor_scalar(rstd[:, :], pm[2][:, 0:T], 1.0 / RET_DIM, EPS, ALU.mult, ALU.add).then_inc(ret_var, 1)

        def ret_inverse(h):
            dve.wait_ge(ret_std, h + 1)
            own(dve.reciprocal(rstd[:, :], rstd[:, :]))

        def ret_gate(h):
            dve.wait_ge(act_done, FB // 2 + h + 1)
            o = pm[1][:, :].rearrange("p (b t) -> p b t", b=2)
            own(dve.tensor_tensor(val[:, 0, :, :], o, rstd[:, :].unsqueeze(1).to_broadcast([P, 2, T]), ALU.mult))
            for b in range(2):
                ins = dve.scalar_tensor_tensor(out=val[:, 0, b, :], in0=val[:, 0, b, :], scalar=col("ret_norm_w_2", 2 * h + b),
                                               in1=g_r[:, 2 * h + b, :], op0=ALU.mult, op1=ALU.mult)
            ins.then_inc(ret_full, 1)

        def ret_low(h):
            dve.wait_ge(ret_hi, h + 1)
            dve.tensor_tensor(o_r[:, 2 * h:2 * h + 2, 1, :], val[:, 0, :, :],
                              o_r[:, 2 * h:2 * h + 2, 0, :].bitcast(F32), ALU.subtract).then_inc(ret_ready, 1)
            dve.wait_ge(ret_ready, h + 1)

        def second_mid(q):
            def mid(c):
                if q == 0 and c == 3:
                    variance(2)
                    dve.wait_ge(std_ready, 3)
                    dve.reciprocal(rstd_h[:, :], rstd_h[:, :]).then_inc(rstd_ready, 1)
                    dve.wait_ge(rstd_ready, 1)
                if q == 1 and c == 0:
                    own(dve.reciprocal(rstd[:, :], rstd[:, :]))
                if 1 <= q <= 8 and c == 2:
                    final_x(q - 1)
                if q == 4 and c == 0:
                    dve.wait_ge(rstd_turned, 1)
                    own(dve.tensor_copy(rstd_col[:, :], pm[3][:, 0:2]))
                if c == 0 and 2 <= q <= 9:
                    rotate_m(q - 2)
                if c == 0 and 0 <= q - 13 < 8:
                    moba_max(q - 13)
                if c == 2 and 0 <= q - 13 < 8:
                    moba_softmax(q - 13)
                if c == 1 and 0 <= q - 16 < 8:
                    moba_low(q - 16)
                if 24 <= q <= 30 and q % 2 == 0 and c == 0:
                    ret_decay((q - 24) // 2)
                if 26 <= q <= 32 and q % 2 == 0:
                    h = (q - 26) // 2
                    if c == 0:
                        ret_variance(h)
                    if c == 1:
                        ret_inverse(h)
                    if c == 2:
                        ret_gate(h)
                    if c == 3:
                        ret_low(h)
            return mid

        for q in range(IN2_SLABS):
            if q < 8:
                dst = qk_m[:, 2 * (q % 4):2 * (q % 4) + 2, q // 4, :]
            elif q < 12:
                dst = v_m[:, :, SLAB * (q - 8):SLAB * (q - 7)]
            elif q < 20:
                dst = qk_r[:, (q - 12) % 4, (q - 12) // 4, :, :]
            elif q < 24:
                dst = v_r[:, :, SLAB * (q - 20):SLAB * (q - 19)]
            elif q < 28:
                dst = g_r[:, 2 * (q - 24):2 * (q - 24) + 2, :]
            else:
                dst = val[:, q % 2, :, :]
            if q >= 30:
                dve.wait_ge(act_done, FB // 2 + 4 + q - 29)
            turn((S_IN2 + q) // 2, q % 2, dst, mid=second_mid(q), scale="columns" if q in V_SLABS else rstd_h)
            if 12 <= q < 20:
                rotate_r((q - 12) % 4, (q - 12) // 4).then_inc(qkv_stored, 1)
            elif q < 28:
                dve.nop().then_inc(qkv_stored, 1)

        for m in range(OUT_SLABS):
            pair, s = (S_MERGE + m) // 2, m % 2
            for c in range(CHUNKS):
                if s == 0:
                    convert(pair, 1, c)
                else:
                    convert(pair + 1, 0, c)
                if c == 1:
                    if m == 0:
                        dve.wait_ge(act_done, FB // 2 + 4 + 16)
                    if m >= 1:
                        dve.wait_ge(merged_ready, m)
                    evacuate(S_MERGE + 2 * m, 0, val[:, 0, :, :])
                    own(dve.tensor_tensor(val[:, 0, :, :], val[:, 0, :, :], sig_r[:, 2 * m:2 * m + 2, :], ALU.mult))
            evacuate(S_MERGE + 2 * m + 1, 1, val[:, 1, :, :])
            own(dve.tensor_tensor(val[:, 1, :, :], val[:, 1, :, :], sig_m[:, 2 * m:2 * m + 2, :], ALU.mult))
            dve.tensor_tensor(val[:, 0, :, :], val[:, 0, :, :], val[:, 1, :, :], ALU.add).then_inc(merged_t, 1)
            dve.wait_ge(merged_hi, m + 1)
            dve.tensor_tensor(h_s[:, 2 * m:2 * m + 2, 1, :], val[:, 0, :, :],
                              h_s[:, 2 * m:2 * m + 2, 0, :].bitcast(F32), ALU.subtract).then_inc(merged_ready, 1)
        offset[0] = OUT_SLABS
        dve.wait_ge(merged_ready, OUT_SLABS)
        own(dve.memset(up_pad[:, :, :, 0:PAD_2], 0.0))
        for q in range(OUT_SLABS):
            residual_turn(S_OUT2 + q, q, None, 3, (S_OUT2 + q) // 2, q % 2, pre=(3, mid_s, col("ffn_norm_w_2", 0, DB)))
        ffn(S_FFN2, 4, None, mid_s=h_s)
        inv_rms(4)
        for j in range(4):
            blocks = out_t[:, 4 * j:4 * j + 4, :]
            dve.tensor_tensor(blocks, blocks, rstd[:, :].unsqueeze(1).to_broadcast([P, 4, T]), ALU.mult).then_inc(out_ready, 1)

    ctx.close()


def chunked(w, kt=KT, order=None):
    k, n = w.shape
    a = w.reshape(k // (kt * P), kt, P, n // SLAB, SLAB).transpose(3, 0, 2, 1, 4)
    if order is not None:
        a = a[order]
    return np.ascontiguousarray(a).reshape(n // SLAB, k // (kt * P), P, kt * SLAB)


def tables():
    f = np.float32
    pos = np.arange(T, dtype=f)

    def angles(dim, theta):
        inv = f(theta) ** (-np.arange(0, dim, 2, dtype=f) / f(dim))
        return (pos[None, :] * inv[:, None].astype(f)).astype(np.float64)

    a = angles(RET_DIM, RET_THETA)
    rope_r = np.stack([np.cos(a), np.sin(a)], axis=1).astype(f)
    a = angles(ROT, MOBA_THETA)
    rope_m = np.stack([np.concatenate([np.cos(a), np.cos(a)]), np.concatenate([-np.sin(a), np.sin(a)])], axis=1).astype(f)
    log_g = np.log1p(-np.exp2(-5.0 - np.arange(RET_HEADS)))
    diff = np.arange(T)[None, :] - np.arange(P)[:, None]
    decay = np.where(diff[:, None, :] >= 0, np.exp(log_g[None, :, None] * np.maximum(diff, 0)[:, None, :]), 0.0)
    decay = (decay * RET_DIM ** -0.5).astype(f)
    causal = np.where(np.arange(P)[None, :] <= np.arange(P)[:, None], BIG, -BIG)
    cmask = np.concatenate([causal, np.full((P, P), BIG), causal], axis=1).astype(f)
    perm = np.roll(np.eye(ROT, dtype=f), ROT // 2, axis=1)
    return {"rope_r": rope_r, "rope_m": rope_m, "decay": decay, "cmask": cmask, "perm": perm,
            "ident": np.eye(P, dtype=f)}


def laid_out(inputs):
    a = {k: np.asarray(v) for k, v in inputs.items()}
    d = tables()
    d["x_fm"] = np.ascontiguousarray(a["x"][0].T)
    rows = [a[name].reshape(-1, P) for name in PARAMS]
    d["params"] = np.ascontiguousarray(np.concatenate(rows, axis=0).T)
    d["w_ada"] = np.ascontiguousarray(a["w_ada"][0][:, :ADA_FIRST * ADA_COLS])
    d["w_ada_late"] = np.ascontiguousarray(
        a["w_ada"][0][:, ADA_FIRST * ADA_COLS:].reshape(D, len(RIDE_PARTS), ADA_COLS // P, P).transpose(0, 1, 3, 2)
    ).reshape(D, len(RIDE_PARTS), ADA_COLS)
    d["w_in"] = chunked(a["w_in"][0], order=IN_ORDER)
    d["w_out"] = chunked(np.concatenate([a["w_out"][0][D_LRU:], a["w_out"][0][:D_LRU]]))
    d["w_rg_a"] = np.ascontiguousarray(a["w_rg_a"][0].reshape(LB, 2, LRU_HEAD, LRU_HEAD).transpose(1, 0, 2, 3))
    d["w_rg_i"] = np.ascontiguousarray(a["w_rg_i"][0].reshape(LB, 2, LRU_HEAD, LRU_HEAD).transpose(1, 0, 2, 3))
    d["w_pool"] = a["w_pool"][0]
    d["w_ffn_gate"] = chunked(a["w_ffn_gate"][0])
    d["w_ffn_up"] = chunked(a["w_ffn_up"][0])
    d["w_in_2"] = chunked(a["w_in_2"][0], order=IN2_ORDER)
    d["w_ret_up_2"] = chunked(a["w_ret_up_2"][0])
    d["w_moba_up_2"] = chunked(a["w_moba_up_2"][0])
    d["w_out_2"] = chunked(a["w_out_2"][0])
    d["w_ffn_a_2"] = chunked(a["w_ffn_up_2"][0][:, :D_FF])
    d["w_ffn_b_2"] = chunked(a["w_ffn_up_2"][0][:, D_FF:])
    for name in ("w_ffn_down", "w_ffn_down_2"):
        at = 0
        for g, n in enumerate(FFN_GROUPS):
            d[f"{name}{g}"] = chunked(a[name][0][at:at + n * SLAB], kt=2 * n // CHUNKS)
            at += n * SLAB
    return d


def kernel(**inputs):
    import concourse.bacc as _bacc
    from concourse.bass_utils import run_bass_kernel_spmd as _run

    nc = _bacc.Bacc("TRN2", target_bir_lowering=False, num_devices=1)
    arrays = {f"in_{k}": np.ascontiguousarray(v) for k, v in laid_out(inputs).items()}
    dram = {k[3:]: nc.dram_tensor(k, v.shape, F32, kind="ExternalInput").ap() for k, v in arrays.items()}
    out = nc.dram_tensor("out_fm", (D, T), F32, kind="ExternalOutput").ap()
    build(nc, dram, out)
    r = _run(nc, [arrays], core_ids=[0])
    return np.ascontiguousarray(np.asarray(r.results[0]["out_fm"]).T)[None]
```
